# Optimizing a Trainium2 kernel written in Bass

```python
import math
import jax, jax.numpy as jnp
from jax import lax
import numpy as np

D_MODEL = 1024
BATCH = 1
SEQ = 512
DEPTH = 1

SSM_HEADS = 16
SSM_HEAD_DIM = 64
SSM_D_INNER = SSM_HEADS * SSM_HEAD_DIM
SSM_GROUPS = 2
SSM_STATE = 128
SSM_CONV_DIM = SSM_D_INNER + 2 * SSM_GROUPS * SSM_STATE
GDN_HEADS = 8
GDN_HEAD_K = 128
GDN_HEAD_V = 128
GDN_K_DIM = GDN_HEADS * GDN_HEAD_K
GDN_V_DIM = GDN_HEADS * GDN_HEAD_V
GDN_QKV_DIM = 2 * GDN_K_DIM + GDN_V_DIM
CONV_K = 4
CHUNK = 64
FFN_HIDDEN = -(-8 * D_MODEL // (3 * 256)) * 256
EPS = 1e-6
IN_SPLIT_SIZES = (SSM_D_INNER, SSM_CONV_DIM, SSM_HEADS,
                  GDN_QKV_DIM, GDN_V_DIM, GDN_HEADS, GDN_HEADS,
                  D_MODEL, D_MODEL)
IN_DIM = sum(IN_SPLIT_SIZES)
IN_SPLIT_IDX = tuple(int(i) for i in np.cumsum(IN_SPLIT_SIZES)[:-1])


def rmsnorm(x, w):
    xf = x.astype(jnp.float32)
    y = xf * lax.rsqrt(jnp.mean(xf * xf, axis=-1, keepdims=True) + EPS)
    return (y * w.astype(jnp.float32)).astype(x.dtype)

def causal_dwconv(u, w):
    c = u.shape[-1]
    return lax.conv_general_dilated(
        u, w[:, None, :].astype(u.dtype), window_strides=(1,),
        padding=[(CONV_K - 1, 0)], dimension_numbers=("NWC", "WIO", "NWC"),
        feature_group_count=c)

def to_chunks(t):
    b, s = t.shape[:2]
    return jnp.moveaxis(t.reshape(b, s // CHUNK, CHUNK, *t.shape[2:]), 1, 0)

def from_chunks(t):
    t = jnp.moveaxis(t, 0, 1)
    return t.reshape(t.shape[0], t.shape[1] * t.shape[2], *t.shape[3:])

def ssd_scan(xdt, a, bm, cm):
    bsz, s = xdt.shape[:2]
    r = SSM_HEADS // SSM_GROUPS
    xdt = xdt.reshape(bsz, s, SSM_GROUPS, r, SSM_HEAD_DIM)
    a = a.reshape(bsz, s, SSM_GROUPS, r)
    causal = jnp.tril(jnp.ones((CHUNK, CHUNK), dtype=bool))[None, :, :, None, None]

    def body(state, inp):
        xc, ac, bc, cc = inp
        acum = jnp.cumsum(ac, axis=1)
        seg = acum[:, :, None] - acum[:, None, :]
        lmat = jnp.exp(jnp.where(causal, seg, -jnp.inf))
        cb = jnp.einsum("bign,bjgn->bijg", cc, bc)
        y_diag = jnp.einsum("bijg,bijgr,bjgrp->bigrp", cb, lmat, xc)
        y_off = jnp.einsum("bign,bgrpn->bigrp", cc, state) * jnp.exp(acum)[..., None]
        decay_end = jnp.exp(acum[:, -1:] - acum)
        new_state = state * jnp.exp(acum[:, -1])[..., None, None] + jnp.einsum(
            "bjgn,bjgr,bjgrp->bgrpn", bc, decay_end, xc)
        return new_state, y_diag + y_off

    state0 = jnp.zeros((bsz, SSM_GROUPS, r, SSM_HEAD_DIM, SSM_STATE), jnp.float32)
    _, y = lax.scan(body, state0, (to_chunks(xdt), to_chunks(a), to_chunks(bm), to_chunks(cm)))
    return from_chunks(y).reshape(bsz, s, SSM_HEADS, SSM_HEAD_DIM)

def mamba2_mixer(z, xbc, dt_raw, conv_w, conv_b, dt_bias, a_log, d_skip, norm_w):
    dtype = z.dtype
    bsz, s = z.shape[:2]
    xbc = jax.nn.silu(causal_dwconv(xbc, conv_w) + conv_b.astype(xbc.dtype))
    xs, bm, cm = jnp.split(xbc.astype(jnp.float32),
                           [SSM_D_INNER, SSM_D_INNER + SSM_GROUPS * SSM_STATE], axis=-1)
    xs = xs.reshape(bsz, s, SSM_HEADS, SSM_HEAD_DIM)
    bm = bm.reshape(bsz, s, SSM_GROUPS, SSM_STATE)
    cm = cm.reshape(bsz, s, SSM_GROUPS, SSM_STATE)
    dt = jax.nn.softplus(dt_raw.astype(jnp.float32) + dt_bias.astype(jnp.float32))
    a = -jnp.exp(a_log.astype(jnp.float32))
    y = ssd_scan(xs * dt[..., None], dt * a, bm, cm)
    y = y + d_skip.astype(jnp.float32)[:, None] * xs
    y = y.reshape(bsz, s, SSM_D_INNER) * jax.nn.silu(z.astype(jnp.float32))
    y = y.reshape(bsz, s, SSM_GROUPS, SSM_D_INNER // SSM_GROUPS)
    y = y * lax.rsqrt(jnp.mean(y * y, axis=-1, keepdims=True) + EPS)
    y = y.reshape(bsz, s, SSM_D_INNER) * norm_w.astype(jnp.float32)
    return y.astype(dtype)

def gdn_scan(q, k, v, g, beta):
    bsz = q.shape[0]
    tril = jnp.tril(jnp.ones((CHUNK, CHUNK), dtype=bool))
    strict = jnp.tril(jnp.ones((CHUNK, CHUNK), dtype=bool), -1)
    eye = jnp.eye(CHUNK, dtype=jnp.float32)

    def body(state, inp):
        qc, kc, vc, gcv, bc = inp
        gc = jnp.cumsum(gcv, axis=1)
        gch = jnp.swapaxes(gc, 1, 2)
        decay = jnp.exp(jnp.where(tril, gch[..., :, None] - gch[..., None, :], -jnp.inf))
        kk = jnp.einsum("bihd,bjhd->bhij", kc, kc)
        amat = jnp.where(strict, kk * decay * jnp.swapaxes(bc, 1, 2)[..., :, None], 0.0)
        rhs = jnp.concatenate([vc * bc[..., None], kc * (bc * jnp.exp(gc))[..., None]], axis=-1)
        rhs = jnp.swapaxes(rhs, 1, 2)
        t = lax.linalg.triangular_solve(eye + amat, rhs, left_side=True, lower=True,
                                        unit_diagonal=True)
        u, w = t[..., :GDN_HEAD_V], t[..., GDN_HEAD_V:]
        v_new = u - jnp.einsum("bhqk,bhkv->bhqv", w, state)
        qk = jnp.einsum("bihd,bjhd->bhij", qc, kc) * decay
        o = (jnp.einsum("bihk,bhkv->bhiv", qc * jnp.exp(gc)[..., None], state)
             + jnp.einsum("bhij,bhjv->bhiv", qk, v_new))
        new_state = state * jnp.exp(gch[..., -1])[..., None, None] + jnp.einsum(
            "bjhk,bhjv->bhkv", kc * jnp.exp(gc[:, -1:] - gc)[..., None], v_new)
        return new_state, jnp.swapaxes(o, 1, 2)

    state0 = jnp.zeros((bsz, GDN_HEADS, GDN_HEAD_K, GDN_HEAD_V), jnp.float32)
    _, o = lax.scan(body, state0, (to_chunks(q), to_chunks(k), to_chunks(v),
                                   to_chunks(g), to_chunks(beta)))
    return from_chunks(o)

def gdn_mixer(qkv, z, a_raw, b_raw, conv_w, a_log, dt_bias, norm_w):
    dtype = z.dtype
    bsz, s = z.shape[:2]
    qkv = jax.nn.silu(causal_dwconv(qkv, conv_w)).astype(jnp.float32)
    q, k, v = jnp.split(qkv, [GDN_K_DIM, 2 * GDN_K_DIM], axis=-1)
    q = q.reshape(bsz, s, GDN_HEADS, GDN_HEAD_K)
    k = k.reshape(bsz, s, GDN_HEADS, GDN_HEAD_K)
    v = v.reshape(bsz, s, GDN_HEADS, GDN_HEAD_V)
    q = q * lax.rsqrt(jnp.sum(q * q, axis=-1, keepdims=True) + EPS) * (GDN_HEAD_K ** -0.5)
    k = k * lax.rsqrt(jnp.sum(k * k, axis=-1, keepdims=True) + EPS)
    beta = jax.nn.sigmoid(b_raw.astype(jnp.float32))
    g = -jnp.exp(a_log.astype(jnp.float32)) * jax.nn.softplus(
        a_raw.astype(jnp.float32) + dt_bias.astype(jnp.float32))
    o = gdn_scan(q, k, v, g, beta)
    o = o * lax.rsqrt(jnp.mean(o * o, axis=-1, keepdims=True) + EPS) * norm_w.astype(jnp.float32)
    o = o * jax.nn.silu(z.astype(jnp.float32).reshape(bsz, s, GDN_HEADS, GDN_HEAD_V))
    return o.reshape(bsz, s, GDN_V_DIM).astype(dtype)

def first_inputs(seed: int = 0) -> dict:
    key = jax.random.key(seed)
    ks = jax.random.split(key, 24)
    f32 = jnp.float32

    def nrm(k, shape, scale):
        return jax.random.normal(k, shape, f32) * scale

    def gain(k, shape):
        return 1.0 + 0.02 * jax.random.normal(k, shape, f32)

    def dt_bias_init(k, shape):
        dt = jnp.exp(jax.random.uniform(k, shape, f32, math.log(1e-3), math.log(1e-1)))
        return dt + jnp.log(-jnp.expm1(-dt))

    return {
        "x": jax.random.normal(ks[0], (BATCH, SEQ, D_MODEL), f32),
        "norm_mix_w": gain(ks[1], (DEPTH, D_MODEL)),
        "w_in": nrm(ks[2], (DEPTH, D_MODEL, IN_DIM), D_MODEL ** -0.5),
        "ssm_conv_w": nrm(ks[3], (DEPTH, CONV_K, SSM_CONV_DIM), CONV_K ** -0.5),
        "ssm_conv_b": nrm(ks[4], (DEPTH, SSM_CONV_DIM), 0.02),
        "ssm_dt_bias": dt_bias_init(ks[5], (DEPTH, SSM_HEADS)),
        "ssm_a_log": jnp.log(jax.random.uniform(ks[6], (DEPTH, SSM_HEADS), f32, 1.0, 16.0)),
        "ssm_d": gain(ks[7], (DEPTH, SSM_HEADS)),
        "ssm_norm_w": gain(ks[8], (DEPTH, SSM_D_INNER)),
        "gdn_conv_w": nrm(ks[9], (DEPTH, CONV_K, GDN_QKV_DIM), CONV_K ** -0.5),
        "gdn_a_log": jnp.log(jax.random.uniform(ks[10], (DEPTH, GDN_HEADS), f32, 1.0, 16.0)),
        "gdn_dt_bias": dt_bias_init(ks[11], (DEPTH, GDN_HEADS)),
        "gdn_norm_w": gain(ks[12], (DEPTH, GDN_HEAD_V)),
        "w_proj_ssm": nrm(ks[13], (DEPTH, SSM_D_INNER, D_MODEL), SSM_D_INNER ** -0.5),
        "w_proj_gdn": nrm(ks[14], (DEPTH, GDN_V_DIM, D_MODEL), GDN_V_DIM ** -0.5),
        "w_out": nrm(ks[15], (DEPTH, D_MODEL, D_MODEL), D_MODEL ** -0.5),
        "norm_ffn_w": gain(ks[16], (DEPTH, D_MODEL)),
        "w_ffn_in": nrm(ks[17], (DEPTH, D_MODEL, 2 * FFN_HIDDEN), D_MODEL ** -0.5),
        "w_ffn_down": nrm(ks[18], (DEPTH, FFN_HIDDEN, D_MODEL), FFN_HIDDEN ** -0.5),
        "final_norm_w": gain(ks[19], (D_MODEL,)),
    }

def first_block(x, norm_mix_w, w_in, ssm_conv_w, ssm_conv_b, ssm_dt_bias, ssm_a_log, ssm_d,
              ssm_norm_w, gdn_conv_w, gdn_a_log, gdn_dt_bias, gdn_norm_w, w_proj_ssm,
              w_proj_gdn, w_out, norm_ffn_w, w_ffn_in, w_ffn_down, final_norm_w):
    for l in range(DEPTH):
        h = rmsnorm(x, norm_mix_w[l])
        proj = h @ w_in[l]
        (ssm_z, ssm_xbc, ssm_dt, gdn_qkv, gdn_z, gdn_a, gdn_b,
         gate_ssm, gate_gdn) = jnp.split(proj, IN_SPLIT_IDX, axis=-1)
        y_ssm = mamba2_mixer(ssm_z, ssm_xbc, ssm_dt, ssm_conv_w[l], ssm_conv_b[l],
                             ssm_dt_bias[l], ssm_a_log[l], ssm_d[l], ssm_norm_w[l])
        y_gdn = gdn_mixer(gdn_qkv, gdn_z, gdn_a, gdn_b, gdn_conv_w[l], gdn_a_log[l],
                          gdn_dt_bias[l], gdn_norm_w[l])
        merged = (jax.nn.sigmoid(gate_ssm) * (y_ssm @ w_proj_ssm[l])
                  + jax.nn.sigmoid(gate_gdn) * (y_gdn @ w_proj_gdn[l]))
        x = x + merged @ w_out[l]
        h = rmsnorm(x, norm_ffn_w[l])
        gate, up = jnp.split(h @ w_ffn_in[l], [FFN_HIDDEN], axis=-1)
        x = x + (jax.nn.silu(gate) * up) @ w_ffn_down[l]
    return rmsnorm(x, final_norm_w)


_first_inputs = first_inputs


def first_inputs(seed=0):
    import zlib

    import numpy as np

    out = dict(_first_inputs(seed))
    spreads = {}
    factors = {'norm_mix_w': 2.779,
     'ssm_conv_b': 4.141,
     'ssm_d': 8.0,
     'ssm_norm_w': 6.076,
     'gdn_norm_w': 8.0,
     'norm_ffn_w': 4.392,
     'final_norm_w': 2.838}
    for name, (base, spread) in spreads.items():
        noise = np.random.default_rng([zlib.crc32(name.encode()), seed]).standard_normal(out[name].shape)
        drawn = base * np.exp(spread * noise) if base else spread * noise
        out[name] = __import__('jax').numpy.asarray(drawn.astype(out[name].dtype))
    for name, factor in factors.items():
        out[name] = (out[name] * factor).astype(out[name].dtype)
    return out


_narrow_inputs = first_inputs


def first_inputs(seed=0):

    out = dict(_narrow_inputs(seed))
    wider = {'ssm_conv_b': 3.7, 'ssm_d': 12.0, 'ssm_norm_w': 7.07, 'final_norm_w': 3.19}
    for name, times in wider.items():
        mean = out[name].mean()
        out[name] = (mean + times * (out[name] - mean)).astype(out[name].dtype)
    return out


HEAD_DIM = 64
RWKV_HEADS = 8
D_RWKV = RWKV_HEADS * HEAD_DIM
DECAY_LORA = 64
ICLR_LORA = 64
DECAY_SCALE = 0.606531
GN_EPS = 64e-5
ATT_HEADS = 8
D_ATT = ATT_HEADS * HEAD_DIM
IDX_HEADS = 8
IDX_DIM = 64
TOPK_MAX = 256
Q_BLOCK = 128
NORM_EPS = 1e-6

N_RWKV_COLS = 3 * D_RWKV + DECAY_LORA + ICLR_LORA + D_RWKV
N_DSA_COLS = 3 * D_ATT + D_ATT + IDX_HEADS * IDX_DIM + IDX_DIM + IDX_HEADS
N_MERGE_COLS = 2 * D_MODEL
N_IN = N_RWKV_COLS + N_DSA_COLS + N_MERGE_COLS
RWKV_SPLITS = (D_RWKV, 2 * D_RWKV, 3 * D_RWKV, 3 * D_RWKV + DECAY_LORA,
               3 * D_RWKV + DECAY_LORA + ICLR_LORA)
DSA_SPLITS = (D_ATT, 2 * D_ATT, 3 * D_ATT, 4 * D_ATT,
              4 * D_ATT + IDX_HEADS * IDX_DIM,
              4 * D_ATT + IDX_HEADS * IDX_DIM + IDX_DIM)


def rms_norm(x, g, eps=NORM_EPS):
    xf = x.astype(jnp.float32)
    y = xf * lax.rsqrt(jnp.mean(xf * xf, axis=-1, keepdims=True) + eps)
    return (y * g.astype(jnp.float32)).astype(x.dtype)

def rwkv7_time_mix(pa, mu, w0, w_up, a0, a_up, k_k, k_a, r_k, gn_w, gn_b):
    B, S, _ = pa.shape
    prev = jnp.pad(pa, ((0, 0), (1, 0), (0, 0)))[:, :S]
    pa = pa + mu * (prev - pa)
    r, k, v, wd, ad, g = jnp.split(pa, RWKV_SPLITS, axis=-1)
    w = jnp.exp(-DECAY_SCALE * jax.nn.sigmoid((w0 + jnp.tanh(wd) @ w_up).astype(jnp.float32)))
    a = jax.nn.sigmoid((a0 + ad @ a_up).astype(jnp.float32))
    kk = (k * k_k).astype(jnp.float32).reshape(B, S, RWKV_HEADS, HEAD_DIM)
    kk = kk / jnp.maximum(jnp.linalg.norm(kk, axis=-1, keepdims=True), 1e-12)
    k = (k * (1.0 + (a - 1.0) * k_a)).astype(jnp.float32)
    hs = lambda t: t.astype(jnp.float32).reshape(B, S, RWKV_HEADS, HEAD_DIM)
    r_h, w_h, k_h, v_h, a_h = hs(r), hs(w), hs(k), hs(v), hs(a)
    b_h = kk * a_h
    tm = lambda t: jnp.moveaxis(t, 1, 0)

    def step(state, inp):
        r_t, w_t, k_t, v_t, nkk_t, b_t = inp
        sa = jnp.einsum('bhvk,bhk->bhv', state, nkk_t)
        state = (state * w_t[:, :, None, :]
                 + sa[..., None] * b_t[:, :, None, :]
                 + v_t[..., None] * k_t[:, :, None, :])
        y_t = jnp.einsum('bhvk,bhk->bhv', state, r_t)
        return state, y_t

    s0 = jnp.zeros((B, RWKV_HEADS, HEAD_DIM, HEAD_DIM), jnp.float32)
    _, y = lax.scan(step, s0, (tm(r_h), tm(w_h), tm(k_h), tm(v_h), tm(-kk), tm(b_h)))
    y = jnp.moveaxis(y, 0, 1)
    mean = jnp.mean(y, axis=-1, keepdims=True)
    var = jnp.mean(jnp.square(y - mean), axis=-1, keepdims=True)
    y = (y - mean) * lax.rsqrt(var + GN_EPS)
    y = y * gn_w.reshape(RWKV_HEADS, HEAD_DIM) + gn_b.reshape(RWKV_HEADS, HEAD_DIM)
    bonus = jnp.sum(r_h * k_h * r_k.astype(jnp.float32), axis=-1, keepdims=True) * v_h
    y = (y + bonus).reshape(B, S, D_RWKV).astype(pa.dtype)
    return y, g

def dsa_sparse_attention(q, k, v, iq, ik, iw):
    B, S, H, Dh = q.shape
    topk = min(TOPK_MAX, S // 4)
    nb = S // Q_BLOCK
    key_chunk = jnp.arange(S) // CHUNK
    ik32 = ik.astype(jnp.float32)
    iw32 = iw.astype(jnp.float32) * (IDX_HEADS ** -0.5)
    blocks = lambda t: jnp.moveaxis(t.reshape((B, nb, Q_BLOCK) + t.shape[2:]), 1, 0)
    q_pos = jnp.arange(S).reshape(nb, Q_BLOCK)
    scale = HEAD_DIM ** -0.5

    def block_fn(args):
        qb, iqb, iwb, pos = args
        q_chunk = pos // CHUNK
        sc = jnp.einsum('bqhd,bsd->bqhs', iqb.astype(jnp.float32), ik32) * (IDX_DIM ** -0.5)
        idx_score = jnp.einsum('bqhs,bqh->bqs', jax.nn.relu(sc), iwb)
        adm = key_chunk[None, :] <= q_chunk[:, None]
        idx_score = jnp.where(adm[None], idx_score, -jnp.inf)
        _, sel = lax.top_k(idx_score, topk)
        valid = (sel // CHUNK) <= q_chunk[None, :, None]
        k_sel = jax.vmap(lambda kb, ib: kb[ib])(k, sel)
        v_sel = jax.vmap(lambda vb, ib: vb[ib])(v, sel)
        logits = jnp.einsum('bqhd,bqkhd->bqhk', qb.astype(jnp.float32),
                            k_sel.astype(jnp.float32)) * scale
        logits = jnp.where(valid[:, :, None, :], logits, -jnp.inf)
        p = jax.nn.softmax(logits, axis=-1)
        return jnp.einsum('bqhk,bqkhd->bqhd', p, v_sel.astype(jnp.float32)).astype(q.dtype)

    out = lax.map(block_fn, (blocks(q), blocks(iq), blocks(iw32), q_pos))
    return jnp.moveaxis(out, 0, 1).reshape(B, S, H, Dh)

def hybrid_layer(x, c, norm_w, w_ada, b_ada, w_in, mu, w0, w_up, a0, a_up, k_k, k_a,
                 r_k, gn_w, gn_b, q_gain, k_gain, w_a_out, w_b_out, w_o):
    B, S, D = x.shape
    mod = jax.nn.silu(c) @ w_ada + b_ada
    shift, scale, gate = jnp.split(mod, 3, axis=-1)
    h = rms_norm(x, norm_w) * (1.0 + scale[:, None, :]) + shift[:, None, :]
    p = h @ w_in
    pa = p[..., :N_RWKV_COLS]
    pb = p[..., N_RWKV_COLS:N_RWKV_COLS + N_DSA_COLS]
    pg = p[..., N_RWKV_COLS + N_DSA_COLS:]
    ya, ga = rwkv7_time_mix(pa, mu, w0, w_up, a0, a_up, k_k, k_a, r_k, gn_w, gn_b)
    ya = (ya * jax.nn.silu(ga)) @ w_a_out
    q, k, v, gb, iq, ik, iw = jnp.split(pb, DSA_SPLITS, axis=-1)
    heads = lambda t: t.reshape(B, S, ATT_HEADS, HEAD_DIM)
    q = rms_norm(heads(q), q_gain)
    k = rms_norm(heads(k), k_gain)
    v = heads(v)
    iq = iq.reshape(B, S, IDX_HEADS, IDX_DIM)
    yb = dsa_sparse_attention(q, k, v, iq, ik, iw).reshape(B, S, D_ATT)
    yb = (yb * jax.nn.silu(gb)) @ w_b_out
    gm_a, gm_b = jnp.split(pg, 2, axis=-1)
    merged = jax.nn.sigmoid(gm_a) * ya + jax.nn.sigmoid(gm_b) * yb
    out = merged @ w_o
    return x + gate[:, None, :] * out

def second_inputs(seed: int = 0) -> dict:
    key = jax.random.key(seed)
    ks = jax.random.split(key, 24)
    nrm = lambda k, shape, s: jax.random.normal(k, shape, jnp.float32) * s
    L = DEPTH
    return {
        "x": nrm(ks[0], (BATCH, SEQ, D_MODEL), 1.0),
        "c": nrm(ks[1], (BATCH, D_MODEL), 1.0),
        "norm_w": 1.0 + nrm(ks[2], (L, D_MODEL), 0.02),
        "w_ada": nrm(ks[3], (L, D_MODEL, 3 * D_MODEL), 0.5 * D_MODEL ** -0.5),
        "b_ada": nrm(ks[4], (L, 3 * D_MODEL), 0.02),
        "w_in": nrm(ks[5], (L, D_MODEL, N_IN), D_MODEL ** -0.5),
        "mu": jax.random.uniform(ks[6], (L, N_RWKV_COLS), jnp.float32),
        "w0": nrm(ks[7], (L, D_RWKV), 0.5),
        "w_up": nrm(ks[8], (L, DECAY_LORA, D_RWKV), 0.5 * DECAY_LORA ** -0.5),
        "a0": nrm(ks[9], (L, D_RWKV), 0.1),
        "a_up": nrm(ks[10], (L, ICLR_LORA, D_RWKV), 0.5 * ICLR_LORA ** -0.5),
        "k_k": 0.85 + nrm(ks[11], (L, D_RWKV), 0.05),
        "k_a": 1.0 + nrm(ks[12], (L, D_RWKV), 0.05),
        "r_k": nrm(ks[13], (L, RWKV_HEADS, HEAD_DIM), 0.1),
        "gn_w": 1.0 + nrm(ks[14], (L, D_RWKV), 0.02),
        "gn_b": nrm(ks[15], (L, D_RWKV), 0.02),
        "q_gain": 1.0 + nrm(ks[16], (L, HEAD_DIM), 0.02),
        "k_gain": 1.0 + nrm(ks[17], (L, HEAD_DIM), 0.02),
        "w_a_out": nrm(ks[18], (L, D_RWKV, D_MODEL), D_RWKV ** -0.5),
        "w_b_out": nrm(ks[19], (L, D_ATT, D_MODEL), D_ATT ** -0.5),
        "w_o": nrm(ks[20], (L, D_MODEL, D_MODEL), D_MODEL ** -0.5),
    }

def second_block(x, c, norm_w, w_ada, b_ada, w_in, mu, w0, w_up, a0, a_up, k_k, k_a,
              r_k, gn_w, gn_b, q_gain, k_gain, w_a_out, w_b_out, w_o):
    for l in range(DEPTH):
        x = hybrid_layer(x, c, norm_w[l], w_ada[l], b_ada[l], w_in[l], mu[l], w0[l],
                         w_up[l], a0[l], a_up[l], k_k[l], k_k[l] * 0.0 + k_a[l] if False else k_a[l],
                         r_k[l], gn_w[l], gn_b[l], q_gain[l], k_gain[l],
                         w_a_out[l], w_b_out[l], w_o[l])
    return x


_first_inputs_2 = second_inputs


def second_inputs(seed=0):
    import zlib

    import numpy as np

    out = dict(_first_inputs_2(seed))
    spreads = {}
    factors = {}
    for name, (base, spread) in spreads.items():
        noise = np.random.default_rng([zlib.crc32(name.encode()), seed]).standard_normal(out[name].shape)
        drawn = base * np.exp(spread * noise) if base else spread * noise
        out[name] = __import__('jax').numpy.asarray(drawn.astype(out[name].dtype))
    for name, factor in factors.items():
        out[name] = (out[name] * factor).astype(out[name].dtype)
    return out


_narrow_inputs_2 = second_inputs


def second_inputs(seed=0):

    out = dict(_narrow_inputs_2(seed))
    wider = {'norm_w': 12.0,
     'b_ada': 6.29,
     'w0': 3.27,
     'w_up': 8.25,
     'a0': 12.0,
     'k_k': 12.0,
     'k_a': 10.31,
     'gn_w': 12.0,
     'gn_b': 12.0,
     'q_gain': 12.0,
     'k_gain': 12.0}
    for name, times in wider.items():
        mean = out[name].mean()
        out[name] = (mean + times * (out[name] - mean)).astype(out[name].dtype)
    return out


D_FF = 2816
A_WIDTH = 512
A_GROUPS = 8
A_GROUP_DIM = A_WIDTH // A_GROUPS
CHUNK_3 = 128
B_HEADS = 8
B_QK_DIM = 64
B_V_DIM = 2 * B_QK_DIM
B_WIDTH = B_HEADS * B_V_DIM
ROPE_THETA = 500000.0
ROT_DIM = B_QK_DIM // 4
LN_EPS = 1e-5
COL_SIZES = (D_MODEL, D_MODEL, 2 * A_WIDTH,
             B_HEADS * 2 * B_QK_DIM, B_HEADS * 2 * B_QK_DIM, B_WIDTH)
IN_COLS = sum(COL_SIZES)
COL_SPLITS = tuple(int(c) for c in np.cumsum(COL_SIZES)[:-1])


def rms_norm_3(x, gain, eps=NORM_EPS):
    xf = x.astype(jnp.float32)
    y = xf * lax.rsqrt(jnp.mean(xf * xf, axis=-1, keepdims=True) + eps)
    return (y * gain.astype(jnp.float32)).astype(x.dtype)

def layer_norm(x, gain, bias, eps=LN_EPS):
    xf = x.astype(jnp.float32)
    mu = jnp.mean(xf, axis=-1, keepdims=True)
    xc = xf - mu
    y = xc * lax.rsqrt(jnp.mean(xc * xc, axis=-1, keepdims=True) + eps)
    return (y * gain.astype(jnp.float32) + bias.astype(jnp.float32)).astype(x.dtype)

def swiglu(h, w_gate, w_up, w_down):
    return (jax.nn.silu(h @ w_gate) * (h @ w_up)) @ w_down

def rope_tables(positions):
    inv = ROPE_THETA ** (-jnp.arange(0, ROT_DIM, 2, dtype=jnp.float32) / ROT_DIM)
    ang = positions.astype(jnp.float32)[..., None] * inv
    return jnp.cos(ang), jnp.sin(ang)

def apply_partial_rope(t, cos, sin):
    half = ROT_DIM // 2
    r1, r2, rest = t[..., :half], t[..., half:ROT_DIM], t[..., ROT_DIM:]
    return jnp.concatenate([r1 * cos - r2 * sin, r2 * cos + r1 * sin, rest], axis=-1)

def gmlp_chunk_mixer(z_uv, ln_g, ln_b, w_s, b_s):
    bsz, seq, _ = z_uv.shape
    z = jax.nn.gelu(z_uv, approximate=False)
    u, v = jnp.split(z, 2, axis=-1)
    v = layer_norm(v, ln_g, ln_b)
    vc = v.reshape(bsz, seq // CHUNK_3, CHUNK_3, A_GROUPS, A_GROUP_DIM)
    causal = jnp.tril(jnp.ones((CHUNK_3, CHUNK_3), dtype=bool))
    w = jnp.where(causal[None], w_s, jnp.zeros_like(w_s))
    f = jnp.einsum('gts,bcsge->bctge', w, vc) + b_s.T[:, :, None]
    return u * f.reshape(bsz, seq, A_WIDTH)

def diff_attention(q, k, v, positions, q_gain, k_gain, lq1, lk1, lq2, lk2, subln_g, lam_init):
    bsz, seq = q.shape[0], q.shape[1]
    out_dtype = v.dtype
    cos, sin = rope_tables(positions)
    cos, sin = cos[:, :, None, None, :], sin[:, :, None, None, :]
    qf = apply_partial_rope(rms_norm_3(q.astype(jnp.float32), q_gain), cos, sin)
    kf = apply_partial_rope(rms_norm_3(k.astype(jnp.float32), k_gain), cos, sin)
    qf = qf * (B_QK_DIM ** -0.5)
    qf = qf.transpose(0, 2, 3, 1, 4)
    kf = kf.transpose(0, 2, 3, 1, 4)
    vf = v.astype(jnp.float32).transpose(0, 2, 1, 3)
    lam = (jnp.exp(jnp.sum(lq1.astype(jnp.float32) * lk1.astype(jnp.float32)))
           - jnp.exp(jnp.sum(lq2.astype(jnp.float32) * lk2.astype(jnp.float32)))
           + lam_init)
    kpos = jnp.arange(seq)

    def block(i):
        start = i * Q_BLOCK
        qb = lax.dynamic_slice_in_dim(qf, start, Q_BLOCK, axis=3)
        s = jnp.einsum('bhmqd,bhmkd->bhmqk', qb, kf)
        qpos = start + jnp.arange(Q_BLOCK)
        mask = kpos[None, :] <= qpos[:, None]
        p = jax.nn.softmax(jnp.where(mask, s, -jnp.inf), axis=-1)
        a = p[:, :, 0] - lam * p[:, :, 1]
        return jnp.einsum('bhqk,bhkd->bhqd', a, vf)

    o = lax.map(block, jnp.arange(seq // Q_BLOCK))
    o = o.transpose(1, 0, 3, 2, 4).reshape(bsz, seq, B_HEADS, B_V_DIM)
    o = rms_norm_3(o, subln_g) * (1.0 - lam_init)
    return o.reshape(bsz, seq, B_WIDTH).astype(out_dtype)

def third_inputs(seed: int = 0) -> dict:
    key = jax.random.key(seed)
    ks = jax.random.split(key, 32)
    f32 = jnp.float32
    L = DEPTH

    def nrm(k, shape, scale):
        return jax.random.normal(k, shape, dtype=f32) * scale

    def gain(k, shape):
        return 1.0 + 0.01 * jax.random.normal(k, shape, dtype=f32)

    return {
        'x': jax.random.normal(ks[0], (BATCH, SEQ, D_MODEL), dtype=f32),
        'positions': jnp.broadcast_to(jnp.arange(SEQ, dtype=jnp.int32), (BATCH, SEQ)),
        'ffn1_norm': gain(ks[1], (L, D_MODEL)),
        'ffn1_w_gate': nrm(ks[2], (L, D_MODEL, D_FF), D_MODEL ** -0.5),
        'ffn1_w_up': nrm(ks[3], (L, D_MODEL, D_FF), D_MODEL ** -0.5),
        'ffn1_w_down': nrm(ks[4], (L, D_FF, D_MODEL), D_FF ** -0.5),
        'mix_norm': gain(ks[5], (L, D_MODEL)),
        'w_in': nrm(ks[6], (L, D_MODEL, IN_COLS), D_MODEL ** -0.5),
        'a_ln_gain': gain(ks[7], (L, A_WIDTH)),
        'a_ln_bias': nrm(ks[8], (L, A_WIDTH), 0.01),
        'a_w_s': nrm(ks[9], (L, A_GROUPS, CHUNK_3, CHUNK_3), 0.5 * CHUNK_3 ** -0.5),
        'a_b_s': gain(ks[10], (L, A_GROUPS, CHUNK_3)),
        'a_w_proj': nrm(ks[11], (L, A_WIDTH, D_MODEL), A_WIDTH ** -0.5),
        'b_q_norm': gain(ks[12], (L, B_QK_DIM)),
        'b_k_norm': gain(ks[13], (L, B_QK_DIM)),
        'b_lambda_q1': nrm(ks[14], (L, B_QK_DIM), 0.1),
        'b_lambda_k1': nrm(ks[15], (L, B_QK_DIM), 0.1),
        'b_lambda_q2': nrm(ks[16], (L, B_QK_DIM), 0.1),
        'b_lambda_k2': nrm(ks[17], (L, B_QK_DIM), 0.1),
        'b_subln': gain(ks[18], (L, B_V_DIM)),
        'b_w_proj': nrm(ks[19], (L, B_WIDTH, D_MODEL), B_WIDTH ** -0.5),
        'w_out': nrm(ks[20], (L, D_MODEL, D_MODEL), D_MODEL ** -0.5),
        'ffn2_norm': gain(ks[21], (L, D_MODEL)),
        'ffn2_w_gate': nrm(ks[22], (L, D_MODEL, D_FF), D_MODEL ** -0.5),
        'ffn2_w_up': nrm(ks[23], (L, D_MODEL, D_FF), D_MODEL ** -0.5),
        'ffn2_w_down': nrm(ks[24], (L, D_FF, D_MODEL), D_FF ** -0.5),
    }

def third_block(x, positions, ffn1_norm, ffn1_w_gate, ffn1_w_up, ffn1_w_down, mix_norm, w_in,
              a_ln_gain, a_ln_bias, a_w_s, a_b_s, a_w_proj, b_q_norm, b_k_norm,
              b_lambda_q1, b_lambda_k1, b_lambda_q2, b_lambda_k2, b_subln, b_w_proj, w_out,
              ffn2_norm, ffn2_w_gate, ffn2_w_up, ffn2_w_down):
    bsz, seq, _ = x.shape
    for l in range(DEPTH):
        lam_init = 0.8 - 0.6 * math.exp(-0.3 * l)
        x = x + 0.5 * swiglu(rms_norm_3(x, ffn1_norm[l]), ffn1_w_gate[l], ffn1_w_up[l], ffn1_w_down[l])
        h = rms_norm_3(x, mix_norm[l])
        z = h @ w_in[l]
        g_a, g_b, z_uv, z_q, z_k, z_v = jnp.split(z, COL_SPLITS, axis=-1)
        y_a = gmlp_chunk_mixer(z_uv, a_ln_gain[l], a_ln_bias[l], a_w_s[l], a_b_s[l])
        q = z_q.reshape(bsz, seq, B_HEADS, 2, B_QK_DIM)
        k = z_k.reshape(bsz, seq, B_HEADS, 2, B_QK_DIM)
        v = z_v.reshape(bsz, seq, B_HEADS, B_V_DIM)
        y_b = diff_attention(q, k, v, positions, b_q_norm[l], b_k_norm[l],
                             b_lambda_q1[l], b_lambda_k1[l], b_lambda_q2[l], b_lambda_k2[l],
                             b_subln[l], lam_init)
        m = jax.nn.sigmoid(g_a) * (y_a @ a_w_proj[l]) + jax.nn.sigmoid(g_b) * (y_b @ b_w_proj[l])
        x = x + m @ w_out[l]
        x = x + 0.5 * swiglu(rms_norm_3(x, ffn2_norm[l]), ffn2_w_gate[l], ffn2_w_up[l], ffn2_w_down[l])
    return x


_first_inputs_3 = third_inputs


def third_inputs(seed=0):
    import zlib

    import numpy as np

    out = dict(_first_inputs_3(seed))
    spreads = {}
    factors = {}
    for name, (base, spread) in spreads.items():
        noise = np.random.default_rng([zlib.crc32(name.encode()), seed]).standard_normal(out[name].shape)
        drawn = base * np.exp(spread * noise) if base else spread * noise
        out[name] = __import__('jax').numpy.asarray(drawn.astype(out[name].dtype))
    for name, factor in factors.items():
        out[name] = (out[name] * factor).astype(out[name].dtype)
    return out


_narrow_inputs_3 = third_inputs


def third_inputs(seed=0):

    out = dict(_narrow_inputs_3(seed))
    wider = {'ffn1_norm': 12.0,
     'mix_norm': 7.63,
     'a_ln_gain': 12.0,
     'a_ln_bias': 12.0,
     'a_b_s': 12.0,
     'b_q_norm': 12.0,
     'b_k_norm': 12.0,
     'b_lambda_q1': 12.0,
     'b_subln': 12.0,
     'ffn2_norm': 12.0}
    for name, times in wider.items():
        mean = out[name].mean()
        out[name] = (mean + times * (out[name] - mean)).astype(out[name].dtype)
    return out


def setup_inputs(seed=0):
    out = dict(first_inputs(seed))
    for name, value in second_inputs(seed + 1).items():
        if name != "x":
            out[name + "_2"] = value
    for name, value in third_inputs(seed + 2).items():
        if name != "x":
            out[name + "_3"] = value
    return out


def reference(
    x, norm_mix_w, w_in, ssm_conv_w, ssm_conv_b, ssm_dt_bias, ssm_a_log, ssm_d, ssm_norm_w,
    gdn_conv_w, gdn_a_log, gdn_dt_bias, gdn_norm_w, w_proj_ssm, w_proj_gdn, w_out, norm_ffn_w,
    w_ffn_in, w_ffn_down, final_norm_w, c_2, norm_w_2, w_ada_2, b_ada_2, w_in_2, mu_2, w0_2,
    w_up_2, a0_2, a_up_2, k_k_2, k_a_2, r_k_2, gn_w_2, gn_b_2, q_gain_2, k_gain_2, w_a_out_2,
    w_b_out_2, w_o_2, positions_3, ffn1_norm_3, ffn1_w_gate_3, ffn1_w_up_3, ffn1_w_down_3,
    mix_norm_3, w_in_3, a_ln_gain_3, a_ln_bias_3, a_w_s_3, a_b_s_3, a_w_proj_3, b_q_norm_3,
    b_k_norm_3, b_lambda_q1_3, b_lambda_k1_3, b_lambda_q2_3, b_lambda_k2_3, b_subln_3,
    b_w_proj_3, w_out_3, ffn2_norm_3, ffn2_w_gate_3, ffn2_w_up_3, ffn2_w_down_3,
):
    x = first_block(
        x, norm_mix_w, w_in, ssm_conv_w, ssm_conv_b, ssm_dt_bias, ssm_a_log, ssm_d, ssm_norm_w,
        gdn_conv_w, gdn_a_log, gdn_dt_bias, gdn_norm_w, w_proj_ssm, w_proj_gdn, w_out,
        norm_ffn_w, w_ffn_in, w_ffn_down, final_norm_w,
    )
    x = second_block(
        x, c_2, norm_w_2, w_ada_2, b_ada_2, w_in_2, mu_2, w0_2, w_up_2, a0_2, a_up_2, k_k_2,
        k_a_2, r_k_2, gn_w_2, gn_b_2, q_gain_2, k_gain_2, w_a_out_2, w_b_out_2, w_o_2,
    )
    return third_block(
        x, positions_3, ffn1_norm_3, ffn1_w_gate_3, ffn1_w_up_3, ffn1_w_down_3, mix_norm_3,
        w_in_3, a_ln_gain_3, a_ln_bias_3, a_w_s_3, a_b_s_3, a_w_proj_3, b_q_norm_3, b_k_norm_3,
        b_lambda_q1_3, b_lambda_k1_3, b_lambda_q2_3, b_lambda_k2_3, b_subln_3, b_w_proj_3,
        w_out_3, ffn2_norm_3, ffn2_w_gate_3, ffn2_w_up_3, ffn2_w_down_3,
    )


_drawn_inputs = setup_inputs


def setup_inputs(seed=0):
    import zlib

    import numpy as np

    out = dict(_drawn_inputs(seed))
    spreads = {}
    factors = {'ssm_d': 3.338,
     'norm_w_2': 2.877,
     'w0_2': 3.382,
     'w_up_2': 3.684,
     'a0_2': 3.372,
     'a_up_2': 7.892,
     'k_k_2': 7.904,
     'r_k_2': 3.453,
     'gn_w_2': 6.388,
     'gn_b_2': 6.539,
     'q_gain_2': 8.0,
     'k_gain_2': 8.0,
     'w_b_out_2': 2.73,
     'ffn1_norm_3': 3.192,
     'mix_norm_3': 3.055,
     'a_ln_gain_3': 8.0,
     'a_ln_bias_3': 8.0,
     'a_b_s_3': 3.826,
     'b_q_norm_3': 6.55,
     'b_k_norm_3': 7.897,
     'b_lambda_q1_3': 64.0,
     'b_lambda_q2_3': 200.0,
     'b_lambda_k2_3': 8.0,
     'b_subln_3': 13.289,
     'ffn2_norm_3': 3.156}
    for name, (base, spread) in spreads.items():
        noise = np.random.default_rng([zlib.crc32(name.encode()), seed]).standard_normal(out[name].shape)
        drawn = base * np.exp(spread * noise) if base else spread * noise
        out[name] = __import__('jax').numpy.asarray(drawn.astype(out[name].dtype))
    for name, factor in factors.items():
        out[name] = (out[name] * factor).astype(out[name].dtype)
    return out
```

```python
import math
import numpy as np
import concourse.bass as bass
from concourse import mybir
from contextlib import ExitStack

F32 = mybir.dt.float32
F32R = mybir.dt.float32r
I32 = mybir.dt.int32
ALU = mybir.AluOpType
ACT = mybir.ActivationFunctionType
AX = mybir.AxisListType
MUL, ADD, SUB, MAX, MIN = ALU.mult, ALU.add, ALU.subtract, ALU.max, ALU.min

NEG = -1.0e30
DECAY_SCALE = 0.606531
LAM_INIT = 0.8 - 0.6 * math.exp(-0.3 * 0)
NFF = 22


def constants():
    i = np.arange(128)
    p, f = i[:, None], i[None, :]
    c = {}
    c["ident"] = (p == f)
    c["ones"] = np.ones((128, 128))
    c["blk"] = (p // 64 == f // 64)
    c["incl"] = (p <= f)
    c["strict"] = (p < f)
    c["nincl"] = np.where(p <= f, 0.0, NEG)
    c["u16"] = (p < f) & (p // 16 == f // 16)
    c["l16"] = (p > f) & (p // 16 == f // 16)
    for b in (16, 32, 64):
        c[f"q{b}"] = (p > f) & (p // b != f // b) & (p // (2 * b) == f // (2 * b))
    c["s64"] = (p < f) & (p // 64 == f // 64)
    c["i64"] = (p <= f) & (p // 64 == f // 64)
    rot = np.zeros((128, 128))
    for b in (0, 64):
        for k in range(8):
            rot[b + 8 + k, b + k] = -1.0
            rot[b + k, b + 8 + k] = 1.0
    c["rot"] = rot
    t = np.arange(512)[None, :]
    c["r128"] = np.broadcast_to(t % 128 != 0, (128, 512))
    c["r64"] = np.broadcast_to(t % 64 != 0, (128, 512))
    c["causal"] = np.concatenate([np.zeros((128, 384)), np.where(f <= p, 0.0, NEG)], axis=1)
    inv = np.float32(500000.0) ** (-np.arange(0, 16, 2, dtype=np.float32) / np.float32(16))
    w = np.zeros((128, 1), np.float32)
    for b in (0, 8, 64, 72):
        w[b:b + 8, 0] = inv
    c["freq"] = w
    at, n = {}, 0
    for k, v in c.items():
        at[k] = (n, n + v.shape[1])
        n += v.shape[1]
    return np.concatenate([np.asarray(v, np.float32) for v in c.values()], axis=1), at


PCOLS = [("norm_mix_w", 8), ("ssm_conv_w", 48), ("ssm_conv_b", 12), ("dtb", 1), ("alog", 1), ("ssm_d", 8),
         ("ssm_norm_w", 8), ("gdn_conv_w", 96), ("gdn_norm_w", 1), ("norm_ffn_w", 8), ("final_norm_w", 8),
         ("c", 8), ("norm_w", 8), ("b_ada", 24), ("mu", 17), ("w0", 4), ("a0", 4), ("k_k", 4), ("k_a", 4),
         ("r_k", 4), ("gn_w", 4), ("gn_b", 4), ("q_gain", 1), ("k_gain", 1), ("ffn1_norm", 8),
         ("mix_norm", 8), ("b_q_norm", 1), ("b_k_norm", 1), ("subln", 1), ("ffn2_norm", 8)]
PAT = {}
_n = 0
for _k, _c in PCOLS:
    PAT[_k] = (_n, _n + _c)
    _n += _c
NPC = _n

WTS = {
    "s_z": (8, 8, 128), "s_xbc": (12, 8, 128), "small": (1, 8, 96), "g_qkv": (24, 8, 128), "g_z": (8, 8, 128),
    "gate_s": (8, 8, 128), "gate_g": (8, 8, 128), "p_ssm": (8, 8, 128), "p_gdn": (8, 8, 128), "w_out": (8, 8, 128),
    "ff_in": (44, 8, 128), "ff_dn": (8, 22, 128),
    "ada": (24, 8, 128), "pa": (17, 8, 128), "qkv2": (12, 8, 128), "gb": (4, 8, 128), "iq": (4, 8, 128),
    "ik": (1, 8, 128), "iw": (1, 8, 8), "gm": (16, 8, 128), "a_out": (8, 4, 128), "b_out": (8, 4, 128),
    "w_o": (8, 8, 128),
    "f1g": (22, 8, 128), "f1u": (22, 8, 128), "f1d": (8, 22, 128), "in3": (48, 8, 128), "a_proj": (8, 4, 128),
    "b_proj": (8, 8, 128), "out3": (8, 8, 128), "f2g": (22, 8, 128), "f2u": (22, 8, 128), "f2d": (8, 22, 128),
}
EXTRA = {"lnp": (128, 2, 512), "bs": (128, 4, 128), "wsT": (128, 8, 128), "lam": (128, 4, 64), "up": (128, 2, 512)}


class Queue:

    def __init__(self, sem, est):
        self.sem, self.n, self.q, self.seen = sem, 0, [], {}
        self.est, self.clock = est, 0.0

    def add(self, fn, after=(), sig=True, ns=600.0):
        waits = []
        at = self.clock
        stack = list(after)
        while stack:
            t = stack.pop()
            if t is None:
                continue
            if isinstance(t, list):
                stack.extend(t)
                continue
            s, v = t
            at = max(at, self.est.get((id(s), v), 0.0) + 180.0)
            if v > 0 and self.seen.get(id(s), 0) < v:
                self.seen[id(s)] = v
                waits = [(a, b) for a, b in waits if a is not s] + [(s, v)]
        self.clock = LAST[0] = at + ns
        if sig:
            self.n += 1
            self.est[(id(self.sem), self.n)] = self.clock
        self.q.append((waits, fn, self.sem if sig else None, 1))
        return (self.sem, self.n)

    def now(self):
        return (self.sem, self.n)

    def emit(self, eng):
        for waits, fn, sem, by in self.q:
            for s, v in waits:
                eng.wait_ge(s, v)
            ins = fn(eng)
            if sem is not None:
                ins.then_inc(sem, by)


class Buf:

    def __init__(self, ap, sem=None, r=None):
        self.a, self.r, self.sem, self.k = ap, r, sem, 0
        self.full, self.empty = None, []


class Pair:

    def __init__(self, hi, lo, t):
        self.hi, self.lo, self.full = hi, lo, t


class Pool:

    def __init__(self, slots):
        self.free = list(slots)

    def take(self):
        while not self.free:
            yield -1.0
        return self.free.pop(0)

    def now(self):
        assert self.free
        return self.free.pop(0)

    def put(self, s, *counts):
        s.full, s.empty = None, list(counts)
        self.free.append(s)


STEP = [0]
LAST = [0.0]


def run(gen):
    idle = 0
    before = STEP[0]
    for _ in gen:
        idle = idle + 1 if STEP[0] == before else 0
        before = STEP[0]
        assert idle < 3000, "no buffer is ever given back"


def v3(ap):
    return ap.rearrange("p (t i) -> p t i", t=4)


def build(nc, D, out):
    const_np, CAT = constants()
    ctx = ExitStack()
    with ctx:
        def sb(name, shape, dt=F32):
            return ctx.enter_context(nc.sbuf_tensor(name, shape, dt))

        def sem(name):
            return ctx.enter_context(nc.semaphore(name))

        sems = [sem(n) for n in ("s_pe", "s_dve", "s_act", "s_pool", "s_sp")]
        banks = [ctx.enter_context(nc.psum_tensor(f"ps{i}", [128, 512], F32))[:, :] for i in range(8)]
        CN = sb("CN", [128, const_np.shape[1]])
        PC = sb("PC", [128, NPC])
        X = sb("X", [128, 8, 512])
        sm = sb("sm", [128, 4096 // 4])
        raws = [(sb(f"W{i}", [128, 1024])[:, :], sem(f"s_w{i}")) for i in range(NW)]
        halves = [sb(f"R{i}", [128, 2048], F32R)[:, :] for i in range(NH)]
        base = -(-nc.sbuf_base // 32) * 32
        sb("tiles", [128, NS * 512])
        tiles = [(nc.alloc_sbuf_tensor_at(f"t{i}", [128, 512], F32, offset=base + 2048 * i)[:, :], sem(f"s_t{i}"),
                  nc.alloc_sbuf_tensor_at(f"u{i}", [128, 512], F32R, offset=base + 2048 * i)[:, :])
                 for i in range(NS)]
        s_c, s_p, s_x, s_o = sem("s_c"), sem("s_p"), sem("s_x"), sem("s_o")
        order = program(nc, D, out, None, sems, banks, CN, PC, X, sm, raws, halves, tiles, CAT,
                        (s_c, s_p, s_x, s_o))[0:2]
        _, _, T, V, A, G, S = program(nc, D, out, order, sems, banks, CN, PC, X, sm, raws, halves, tiles, CAT,
                                   (s_c, s_p, s_x, s_o))

        block = ctx.enter_context(nc.Block())

        @block.sync
        def _(eng):
            S.emit(eng)
            eng.wait_ge(s_o, 16)

        @block.tensor
        def _(eng):
            T.emit(eng)

        @block.vector
        def _(eng):
            V.emit(eng)

        @block.scalar
        def _(eng):
            A.emit(eng)

        @block.gpsimd
        def _(eng):
            G.emit(eng)


NW, NH, NS, AHEAD = 3, 3, 67, 2
NG = 6


def program(nc, D, out, order, sems, banks, CN, PC, X, sm, raws, halves, tiles, CAT, once):
    if True:
        est = {}
        T, V, A, G, S = (Queue(x, est) for x in sems)
        picks = [] if order is None else list(order[1])
        order = None if order is None else order[0]
        dry = order is None
        s_c, s_p, s_x, s_o = once
        PS = Pool([Buf(b) for b in banks])
        WR = Pool([Buf(a, x) for a, x in raws])
        HL = Pool([Buf(None, None, r) for r in halves])
        SP = Pool([Buf(a, x, r) for a, x, r in tiles])

        class Small:
            n = 0

        def small(k):
            Small.n += k
            assert Small.n <= 1024
            return sm[:, Small.n - k:Small.n]

        def C(name):
            a, b = CAT[name]
            return CN[:, a:b]

        def P(name, j=0):
            return PC[:, PAT[name][0] + j:PAT[name][0] + j + 1]

        def step():
            STEP[0] += 1

        def size(ap):
            n = 1
            for x in ap.shape[1:]:
                n *= x
            return n

        SETS = {ACT.Exp: 1, ACT.Ln: 2, ACT.Sqrt: 5, ACT.Gelu: 6, ACT.Sin: 7,
                ACT.Tanh: 1}
        table = [0]

        def mm(o, l, r, start, stop, after=(), sig=None):
            step()
            n = size(r) / 2.4
            return T.add(lambda e: e.matmul(o, l, r, start=start, stop=stop), after, stop if sig is None else sig,
                         n + 3 if r.dtype == F32R else 4 * n)

        def tp(o, i, after=(), sig=True, n=128):
            step()
            return T.add(lambda e: e.transpose(o, i, C("ident")[0:n, 0:n]), after, sig, 107.0)

        def cost(o, E=None):
            return size(o) / 0.96 + 60 if E is None or E is V else size(o) * 2.0 + 60

        def tt(o, a, b, op, after=(), E=None):
            step()
            return (E or V).add(lambda e: e.tensor_tensor(o, a, b, op), after, ns=cost(o, E))

        def ts(o, a, s1, s2=None, op0=MUL, op1=None, after=(), E=None):
            step()
            if op1 is None:
                return (E or V).add(lambda e: e.tensor_scalar(o, a, s1, None, op0), after, ns=cost(o))
            return (E or V).add(lambda e: e.tensor_scalar(o, a, s1, s2, op0, op1), after,
                                  ns=cost(o))

        def stt(o, a, s, b, op0, op1, after=()):
            step()
            return V.add(lambda e: e.scalar_tensor_tensor(out=o, in0=a, scalar=s, in1=b, op0=op0, op1=op1), after,
                         ns=cost(o))

        def act(o, i, f, after=(), **kw):
            step()
            ns = size(o) / 1.2 + 190
            if f in SETS and SETS[f] != table[0]:
                table[0] = SETS[f]
                ns += 1283
            return A.add(lambda e: e.activation(o, i, f, **kw), after, ns=ns)

        def tanh_half(o, i, after, bias=None):
            if bias is None:
                return act(o, i, ACT.Tanh, after, scale=0.5)
            return act(o, i, ACT.Tanh, after, scale=0.5, bias=bias)

        def silu2(o, i, after):
            t = tanh_half(o, i, after)
            return stt(o, o, 1.0, i, ADD, MUL, [t])

        def cp(o, i, after=(), E=None):
            step()
            if E is V:
                return V.add(lambda e: e.tensor_copy(o, i), after, ns=cost(o))
            return act(o, i, ACT.Copy, after)

        def load(slot, dst, src):
            step()
            slot.k += 16
            S.add(lambda e, s=slot.sem: e.dma_start(dst, src).then_inc(s, 16) and None or None, slot.empty, sig=False)
            slot.full = (slot.sem, slot.k)
            return slot.full

        S.q.append(([], lambda e: e.dma_start(PC[:, :], D["params"]), s_p, 16))
        S.q.append(([], lambda e: e.dma_start(X[:, :, :], D["x"]), s_x, 16))
        S.q.append(([], lambda e: e.dma_start(CN[:, :], D["consts"]), s_c, 16))
        tC, tP, tX = (s_c, 16), (s_p, 16), (s_x, 16)
        half, tH = {}, None
        for k in ("ssm_conv_w", "ssm_conv_b", "gdn_conv_w", "w0", "a0", "k_a"):
            a0, a1 = PAT[k]
            half[k] = small(a1 - a0)
            tH = ts(half[k], PC[:, a0:a1], 0.5, None, MUL, None, [tP])

        def HP(name, j):
            return half[name][:, j:j + 1]

        asked, loaded, ready = [], [], []

        def fetch(key):
            name, j, k0, k1, cols = key
            w = WR.now()
            w.n = (k1 - k0) * cols
            load(w, w.a[:, 0:w.n], D[name][j, :, k0:k1, :].rearrange("p k n -> p (k n)"))
            loaded.append(w)

        def split_panel(key):
            w = loaded[len(ready)]
            if key[0] == "ada":
                ready.append(w)
                return
            r = HL.now()
            hi, lo = r.r[:, 0:w.n], r.r[:, 1024:1024 + w.n]
            t = act(hi, w.a[:, 0:w.n], ACT.Copy, [w.full, r.empty])
            r.full = [t, tt(lo, w.a[:, 0:w.n], hi.bitcast(F32), SUB, [w.full, t, r.empty], G)]
            if dry:
                for k in r.full:
                    est[(id(k[0]), k[1])] = 0.0
            WR.put(w, A.now(), G.now())
            ready.append(r)

        def panel(name, j, k0, k1, cols):
            key = (name, j, k0, k1, cols)
            n = len(asked)
            asked.append(key)
            todo = asked if order is None else order
            assert todo[n] == key
            ahead = 0 if order is None else AHEAD
            while len(ready) < min(n + 1 + ahead, len(todo)):
                if len(ready) > n and not (HL.free and (WR.free or len(loaded) > len(ready))):
                    break
                if len(loaded) == len(ready):
                    fetch(todo[len(loaded)])
                split_panel(todo[len(ready)])
            while WR.free and len(loaded) < (len(todo) if order is not None else 0):
                fetch(todo[len(loaded)])
            w = ready[n]
            m = (k1 - k0) * cols
            if name == "ada":
                return w, w.a[:, 0:m].rearrange("p (k n) -> p k n", n=cols), None
            return (w, w.r[:, 0:m].rearrange("p (k n) -> p k n", n=cols),
                    w.r[:, 1024:1024 + m].rearrange("p (k n) -> p k n", n=cols))

        def split(x, after, E=None):
            hi = yield from SP.take()
            lo = yield from SP.take()
            t = act(hi.r, x, ACT.Copy, [after, hi.empty])
            t2 = tt(lo.r, x, hi.r.bitcast(F32), SUB, [after, t, lo.empty], E)
            return Pair(hi, lo, [t, t2])

        def put_pair(p, *q):
            SP.put(p.hi, *q)
            SP.put(p.lo, *q)

        def to_pair(s):
            p = yield from split(s.a, s.full)
            SP.put(s, A.now(), V.now())
            yield
            return p

        def dense(name, j, rhs):
            _, KT, cols = WTS[name]
            while DL[0] or not PS.free:
                yield -1.0
            DL[0] = True
            b = PS.now()
            for k0 in range(0, KT, 8):
                k1 = min(k0 + 8, KT)
                w, wh, wl = panel(name, j, k0, k1, cols)
                for k in range(k0, k1):
                    x = rhs(k)
                    mm(b.a[0:cols, :], wh[:, k - k0, :], x.hi.r, k == 0, False, [w.full, x.full, b.empty])
                    mm(b.a[0:cols, :], wh[:, k - k0, :], x.lo.r, False, False)
                    t = mm(b.a[0:cols, :], wl[:, k - k0, :], x.hi.r, False, k == KT - 1, sig=(k == k1 - 1))
                    if k % 2 and k < k1 - 1:
                        yield
                HL.put(w, T.now())
            DL[0] = False
            b.full = t
            yield
            return b

        DL = [False]

        def by_token(name, j, func=ACT.Copy):
            b = yield from dense(name, j, hk)
            x = yield from SP.take()
            x.full = act(x.a, b.a, func, [b.full, x.empty])
            PS.put(b, A.now())
            yield
            b = yield from transpose4(x.a, x.full)
            SP.put(x, T.now())
            return b

        HS = []

        def norm_h(w, shift=None):
            for p in HS:
                put_pair(p, T.now())
            HS.clear()
            r = yield from inv_rms(xk, tXX[0])
            last = None
            for k in range(9):
                if k < 8:
                    h = yield from SP.take()
                    h.full = stt(h.a, xk(k), w(k), r.a, MUL, MUL, [r.full, tP, h.empty, tXX[0]])
                    if shift is not None:
                        h.full = ts(h.a, h.a, shift(k), None, ADD, None, [h.full])
                if last is not None:
                    E = G if k % 2 == 0 else None
                    HS.append((yield from split(last.a, last.full, E)))
                    SP.put(last, A.now(), (E or V).now())
                last = h
            PS.put(r, V.now())
            yield

        def hk(k):
            return HS[k]

        def xk(k):
            return X[:, k, :]

        def rsq(o, ps, scale, eps, mult, after):
            t = ts(o, ps, scale, eps, MUL, ADD, after)
            t = V.add(lambda e: e.reciprocal(o, o), [t])
            return act(o, o, ACT.Sqrt, [t], scale=mult * mult)

        def colsum(mat, tiles, after):
            b = yield from PS.take()
            for i, x in enumerate(tiles):
                q = yield from SP.take()
                t = act(q.a, x, ACT.Square, [after, q.empty])
                yield
                b.full = mm(b.a, C(mat), q.a, i == 0, i == len(tiles) - 1, [tC, t, b.empty], sig=True)
                SP.put(q, T.now())
            yield
            return b

        def token_sum(b, q, n, first, last, after):
            for m in range(4):
                one = C("blk")[:, 0:128:64] if n == 2 else C("ones")[:, 0:1]
                o, l = b.a[:, m * n:m * n + n], q[:, m * 128:m * 128 + 128]
                step()
                b.full = T.add(lambda e, o=o, l=l, one=one, m=m: e.matmul(o, l, one, start=first and m == 0,
                            stop=last and m == 3, skip_group_check=True), [after, b.empty], m == 3, 60.0)
            return b.full

        def token_squares(n, tiles, after):
            b = yield from PS.take()
            for i, x in enumerate(tiles):
                q = yield from SP.take()
                t = act(q.a, x, ACT.Square, [after, q.empty])
                yield
                token_sum(b, q.a, n, i == 0, i == len(tiles) - 1, [tC, t])
                SP.put(q, T.now())
            return b

        def newton(x, xc, y, w, after, mult):
            big = 3.4028234e38
            t = ts(xc, x, big, None, MIN, None, [after])
            t = ts(y.bitcast(I32), xc.bitcast(I32), 1, None, ALU.logical_shift_right, None, [t])
            t = ts(y.bitcast(I32), y.bitcast(I32), -1, 0x5F3759DF, MUL, ADD, [t])
            for i in range(3):
                t = tt(w, y, xc, MUL, [t])
                t = stt(w, w, -0.5, y, MUL, MUL, [t])
                t = stt(y, w, 1.5, y, ADD, MUL, [t])
            t = stt(y, x, big, y, ALU.is_le, MUL, [t])
            if mult != 1.0:
                t = ts(y, y, mult, None, MUL, None, [t])
            return t

        def spread(b, n, scale, eps, mult=1.0, floor=None):
            c = yield from SP.take()
            k = 4 * n
            x, xc, y, w = (c.a[:, i * k:i * k + k] for i in range(4))
            if floor is None:
                t = ts(x, b.a[:, 0:k], scale, eps, MUL, ADD, [b.full, c.empty])
            else:
                t = ts(x, b.a[:, 0:k], floor, None, MAX, None, [b.full, c.empty])
            t = newton(x, xc, y, w, t, mult)
            yield
            for m in range(4):
                for h in range(n):
                    M = 128 // n
                    b.full = mm(b.a[h * M:h * M + M, m * 128:m * 128 + 128],
                             y[:, m * n + h:m * n + h + 1].to_broadcast([128, M]), C("ident"), True, True, [t, tC])
            SP.put(c, T.now())
            yield
            return b

        def inv_rms(src, after):
            if XS:
                b = XS.pop()
                yield
            else:
                b0 = yield from PS.take()
                for k in range(8):
                    q = yield from SP.take()
                    t = act(q.a, src(k), ACT.Square, [after, q.empty])
                    b0.full = mm(b0.a[0:1, :], C("ones")[:, 0:1], q.a, k == 0, k == 7, [tC, t, b0.empty], sig=True)
                    SP.put(q, T.now())
                q = yield from SP.take()
                t = cp(q.a[0:1, :], b0.a[0:1, :], [b0.full, q.empty])
                PS.put(b0, A.now())
                yield
                b = yield from PS.take()
                for m in range(4):
                    b.full = mm(b.a[:, m:m + 1], q.a[0:1, m * 128:m * 128 + 128], C("ones")[0:1, 0:1], True, True,
                             [t, b.empty])
                SP.put(q, T.now())
            b = yield from spread(b, 1, 1.0 / 1024, 1e-6)
            return b

        def transpose4(src, after, n=128):
            b = yield from PS.take()
            for t in range(4):
                b.full = tp(b.a[:, t * 128:(t + 1) * 128], src[:, t * 128:(t + 1) * 128], [tC, after, b.empty])
            yield
            return b

        def bc(ap, row, n, after):
            b = yield from PS.take()
            b.full = mm(b.a, C("ident")[0:n, row:row + 1].to_broadcast([n, 128]), ap[0:n, :], True, True,
                     [tC, after, b.empty])
            yield
            return b

        def invert(U, tU, levels):
            def quad(o, l, r, after):
                for t in range(4):
                    s = slice(t * 128, (t + 1) * 128)
                    k = mm(o.a[:, s], l.a[:, s], r.a[:, s], True, True, [after, o.empty])
                o.full = k
                return k

            def mask(o, i, m, after, E=None):
                return tt(v3(o.a), v3(i.a), C(m).unsqueeze(1).broadcast_to([128, 4, 128]), MUL, [after, o.empty], E)

            yield
            b = yield from transpose4(U.a, tU)
            L = yield from SP.take()
            L.full = cp(L.a, b.a, [b.full, L.empty])
            PS.put(b, A.now())
            d = yield from SP.take()
            e = yield from SP.take()
            d.full = mask(d, U, "u16", [tU], G)
            e.full = mask(e, L, "l16", [L.full])
            p = yield from SP.take()
            p.full = tt(v3(p.a), C("ident").unsqueeze(1).broadcast_to([128, 4, 128]), v3(d.a), SUB, [d.full, p.empty])
            yield
            for lev in range(3):
                b1 = yield from PS.take()
                quad(b1, d, e, [d.full, e.full])
                e2 = yield from SP.take()
                e2.full = cp(e2.a, b1.a, [b1.full, e2.empty])
                PS.put(b1, A.now())
                if lev < 2:
                    b2 = yield from PS.take()
                    quad(b2, e, d, [d.full, e.full])
                    d2 = yield from SP.take()
                    d2.full = cp(d2.a, b2.a, [b2.full, d2.empty], V)
                    PS.put(b2, V.now())
                    SP.put(d, T.now(), V.now())
                    d = d2
                SP.put(e, T.now())
                e = e2
                yield
                b3 = yield from PS.take()
                quad(b3, e, p, [e.full, p.full])
                p.full = tt(p.a, p.a, b3.a, ADD, [b3.full])
                PS.put(b3, V.now())
                yield
            SP.put(e, T.now())
            b = yield from transpose4(p.a, p.full)
            pt = yield from SP.take()
            pt.full = cp(pt.a, b.a, [b.full, pt.empty])
            PS.put(b, A.now())
            yield
            SP.put(d, T.now(), V.now())
            for n, lev in enumerate(levels):
                q = yield from SP.take()
                q.full = mask(q, L, f"q{lev}", [L.full], G)
                b = yield from PS.take()
                quad(b, q, p, [q.full, p.full])
                y = yield from SP.take()
                y.full = cp(y.a, b.a, [b.full, y.empty], V)
                PS.put(b, V.now())
                SP.put(q, T.now())
                yield
                last = n == len(levels) - 1
                b = yield from PS.take()
                quad(b, pt, y, [y.full, pt.full])
                if not last:
                    b2 = yield from PS.take()
                    quad(b2, y, pt, [y.full, pt.full])
                p.full = tt(p.a, p.a, b.a, SUB, [b.full])
                PS.put(b, V.now())
                if not last:
                    pt.full = tt(pt.a, pt.a, b2.a, SUB, [b2.full])
                    PS.put(b2, V.now())
                SP.put(y, T.now())
                yield
            SP.put(L, V.now(), G.now())
            SP.put(pt, T.now())
            return p

        def conv(b, wname, j, nt, o, bias=None):
            def w(k):
                return HP(wname, k * nt + j)
            c = yield from SP.take()
            if bias is None:
                t = ts(c.a, b.a, w(3), None, MUL, None, [b.full, c.empty, tH])
            else:
                t = ts(c.a, b.a, w(3), bias, MUL, ADD, [b.full, c.empty, tH])
            for s in (1, 2, 3):
                t = stt(c.a[:, s:512], b.a[:, 0:512 - s], w(3 - s), c.a[:, s:512], MUL, ADD, [t])
            PS.put(b, V.now())
            t = act(o.a, c.a, ACT.Tanh, [t, o.empty])
            o.full = stt(o.a, o.a, 1.0, c.a, ADD, MUL, [t])
            SP.put(c, V.now())
            yield

        M = [None] * 8

        def gate(name, j, into):
            g = yield from dense(name, j, hk)
            sg = yield from SP.take()
            sg.full = tanh_half(sg.a, g.a, [g.full, sg.empty])
            PS.put(g, A.now())
            into[j % 8] = sg

        def branch(name, gname, y, add, gofs=0, gates=None):
            gates = gates or [None] * 8
            for j in range(8):
                if gates[j] is None:
                    yield from gate(gname, j + gofs, gates)
                sg = gates[j]
                t = sg.full
                b = yield from dense(name, j, lambda k: y[k])
                if add:
                    t = stt(sg.a, sg.a, 1.0, b.a, ADD, MUL, [b.full, t])
                    t = tt(M[j].a, M[j].a, sg.a, ADD, [t, M[j].full])
                    M[j].full = t
                    SP.put(sg, V.now())
                else:
                    sg.full = stt(sg.a, sg.a, 1.0, b.a, ADD, MUL, [b.full, t])
                    M[j] = sg
                PS.put(b, V.now())
            for s in y:
                put_pair(s, T.now())

        XS = []

        def residual(name, y, scale=None, col=None, sq=True):
            qs = []
            if sq:
                b2 = yield from PS.take()
                b2.full = None
            for j in range(8):
                b = yield from dense(name, j, lambda k: y[k])
                if scale is None and col is None:
                    t = tt(X[:, j, :], X[:, j, :], b.a, ADD, [b.full, tXX[0]])
                else:
                    t = stt(X[:, j, :], b.a, scale if col is None else col(j), X[:, j, :], MUL, ADD, [b.full, tXX[0]])
                PS.put(b, V.now())
                if sq:
                    q = yield from SP.take()
                    tq = act(q.a, X[:, j, :], ACT.Square, [t, q.empty])
                    qs.append((q, tq))
                    while len(qs) > (2 if j < 7 else 0):
                        n = j + 1 - len(qs)
                        q, tq = qs.pop(0)
                        token_sum(b2, q.a, 1, n == 0, n == 7, [tq, tC])
                        SP.put(q, T.now())
            if sq:
                XS.append(b2)
            for s in y:
                put_pair(s, T.now())
            tXX[0] = [t, V.now()]

        def merge(name, col=None):
            y = []
            for m in M:
                y.append((yield from to_pair(m)))
            yield from residual(name, y, 0.5 if col is None else None, col=col)

        tXX = [tX]

        def ffn(norm, wg, og, wu, ou, wd, scale, sq=True):
            yield from norm_h(lambda k: P(norm, k))
            hid = []
            for j in range(NFF):
                g = yield from dense(wg, og + j, hk)
                s = yield from SP.take()
                t = silu2(s.a, g.a, [g.full, s.empty])
                PS.put(g, V.now())
                u = yield from dense(wu, ou + j, hk)
                s.full = stt(s.a, s.a, 0.5, u.a, MUL, MUL, [u.full, t])
                PS.put(u, V.now())
                hid.append((yield from to_pair(s)))
            yield from residual(wd, hid, scale, sq=sq)

        def sums():
            b = yield from dense("small", 0, hk)
            sp = yield from SP.take()
            e = yield from SP.take()
            u = yield from SP.take()
            z = yield from SP.take()
            cum = yield from SP.take()
            R = slice(0, 64)
            t = ts(z.a[R], b.a[R], P("dtb")[R], None, ADD, None, [b.full, z.empty, tP])
            t1 = ts(u.a[R], z.a[R], -1.0, None, MUL, None, [t, u.empty])
            t1 = tt(u.a[R], u.a[R], z.a[R], MIN, [t1])
            t2 = act(e.a[R], u.a[R], ACT.Exp, [t1, e.empty])
            t3 = ts(u.a[R], e.a[R], 1.0, None, ADD, None, [t2])
            t4 = act(sp.a[R], u.a[R], ACT.Ln, [t3, sp.empty])
            t5 = ts(u.a[R], u.a[R], 1.0, None, SUB, None, [t4])
            t6 = ts(cum.a[R], u.a[R], 0.0, None, ALU.is_equal, None, [t5, cum.empty])
            t7 = tt(u.a[R], u.a[R], cum.a[R], ADD, [t6])
            t7 = V.add(lambda e_: e_.reciprocal(u.a[R], u.a[R]), [t7])
            t8 = tt(sp.a[R], sp.a[R], u.a[R], MUL, [t7, t4])
            t8 = tt(sp.a[R], sp.a[R], cum.a[R], ADD, [t8])
            t8 = tt(sp.a[R], sp.a[R], e.a[R], MUL, [t8])
            t9 = stt(sp.a[R], z.a[R], 0.0, sp.a[R], MAX, ADD, [t8])
            al = small(1)
            t10 = act(al[R], P("alog")[R], ACT.Exp, [tP])
            t11 = ts(u.a[R], sp.a[R], al[R], -1.0, MUL, MUL, [t9, t10])
            V.add(lambda e_: e_.tensor_tensor_scan(cum.a[R], C("r128")[R], u.a[R], 0.0, MUL, ADD), [t11, tC])
            cum.full = V.now()
            t = tanh_half(cum.a[64:96], b.a[64:96], [b.full, cum.empty, cum.full])
            t = ts(cum.a[64:96], cum.a[64:96], 0.5, 0.5, MUL, ADD, [t])
            PS.put(b, V.now(), A.now())
            cum.full = [cum.full, t]
            SP.put(e, V.now())
            SP.put(u, V.now())
            SP.put(z, V.now())
            tm = yield from SP.take()
            yield
            b = yield from PS.take()
            for t in range(4):
                b.full = tp(b.a[:, t * 96:(t + 1) * 96], cum.a[0:96, t * 128:(t + 1) * 128], [cum.full, b.empty, tC], n=96)
            tm.full = cp(tm.a[:, 0:384], b.a[:, 0:384], [b.full, tm.empty])
            PS.put(b, A.now())
            b = yield from PS.take()
            for t in range(4):
                b.full = tp(b.a[:, t * 16:(t + 1) * 16], sp.a[0:16, t * 128:(t + 1) * 128], [t9, b.empty], n=16)
            t = cp(tm.a[:, 384:448], b.a[:, 0:64], [b.full, tm.full])
            PS.put(b, A.now())
            SP.put(sp, T.now())
            tm.full = [tm.full, t]
            yield
            lst = yield from SP.take()
            b = yield from PS.take()
            b.full = mm(b.a[:, 0:384], C("ident")[:, 127:128].to_broadcast([128, 128]), tm.a[:, 0:384], True, True,
                     [tm.full, b.empty])
            lst.full = cp(lst.a[:, 0:384], b.a[:, 0:384], [b.full, lst.empty])
            PS.put(b, A.now())
            ex = yield from SP.take()
            t = tt(ex.a[:, 0:384], lst.a[:, 0:384], tm.a[:, 0:384], SUB, [lst.full, tm.full, ex.empty])
            ex.full = act(ex.a[:, 0:384], ex.a[:, 0:384], ACT.Exp, [t])
            lst.full = act(lst.a[:, 0:384], lst.a[:, 0:384], ACT.Exp, [lst.full, V.now()])
            ec = yield from SP.take()
            ec.full = act(ec.a[:, 0:384], tm.a[:, 0:384], ACT.Exp, [tm.full, ec.empty])
            K.update(cum=cum, tm=tm, last=lst, end=ex, ecum=ec)

        K = {}

        def cols(name, r0, r1):
            return K[name].a[:, 0:384].rearrange("p (t c) -> p t c", t=4)[:, :, r0:r1]

        def ssm():
            xs, Bf, Cf = [], [], []

            def convs():
                for j in range(12):
                    b = yield from dense("s_xbc", j, hk)
                    o = yield from SP.take()
                    yield from conv(b, "ssm_conv_w", j, 12, o, bias=HP("ssm_conv_b", j))
                    (xs if j < 8 else Bf if j < 10 else Cf).append(o)

            yield from both(sums(), convs())
            cum, tm = K["cum"], K["tm"]
            dt = tm.a[:, 384:448].rearrange("p (t c) -> p t c", t=4)
            xd = []
            for f in range(8):
                b = yield from transpose4(xs[f].a, xs[f].full)
                o = yield from SP.take()
                for hh in range(2):
                    sl = slice(64 * hh, 64 * hh + 64)
                    o.full = tt(v3(o.a)[:, :, sl], v3(b.a)[:, :, sl],
                             dt[:, :, 2 * f + hh:2 * f + hh + 1].broadcast_to([128, 4, 64]), MUL,
                             [b.full, o.empty, tm.full])
                PS.put(b, V.now())
                xd.append(o)
            ys = [None] * 8
            for g in range(2):
                b = yield from transpose4(Bf[g].a, Bf[g].full)
                bt = yield from SP.take()
                bt.full = cp(bt.a, b.a, [b.full, bt.empty])
                PS.put(b, A.now())
                b = yield from PS.take()
                for t in range(4):
                    s = slice(t * 128, t * 128 + 128)
                    b.full = mm(b.a[:, s], Bf[g].a[:, s], Cf[g].a[:, s], True, True, [Bf[g].full, Cf[g].full, b.empty])
                cb = yield from SP.take()
                cb.full = cp(cb.a, b.a, [b.full, cb.empty])
                PS.put(b, A.now())
                SP.put(Bf[g], T.now())
                st = [None]
                for t in range(3):
                    xe = yield from SP.take()
                    for f in range(4):
                        for hh in range(2):
                            h = 8 * g + 2 * f + hh
                            te = ts(xe.a[:, f * 128 + hh * 64:f * 128 + hh * 64 + 64],
                                    v3(xd[4 * g + f].a)[:, t, hh * 64:hh * 64 + 64],
                                    cols("end", h, h + 1)[:, t, :], None, MUL, None,
                                    [xd[4 * g + f].full, K["end"].full, xe.empty])
                    yield
                    b = yield from PS.take()
                    b.full = mm(b.a, v3(bt.a)[:, t, :], xe.a, True, True, [bt.full, te, b.empty])
                    SP.put(xe, T.now())
                    s = yield from SP.take()
                    if t == 0:
                        s.full = cp(s.a, b.a, [b.full, s.empty], V)
                    else:
                        s8 = s.a.rearrange("p (h q) -> p h q", h=8)
                        tk = tt(s8, st[t].a.rearrange("p (h q) -> p h q", h=8),
                                cols("last", 8 * g, 8 * g + 8)[:, t, :].unsqueeze(2).broadcast_to([128, 8, 64]),
                                MUL, [st[t].full, K["last"].full, s.empty])
                        s.full = tt(s.a, s.a, b.a, ADD, [tk, b.full])
                    PS.put(b, V.now())
                    st.append(s)
                    yield
                SP.put(bt, T.now())
                def channel(f, g=g, st=st, cb=cb):
                    F = 4 * g + f
                    ms, cs = [], []
                    for hh in range(2):
                        h = 8 * g + 2 * f + hh
                        bA = yield from bc(cum.a, h, 64, cum.full)
                        m = yield from SP.take()
                        tk = tt(v3(m.a), v3(bA.a), cols("tm", h, h + 1).broadcast_to([128, 4, 128]), SUB,
                                [bA.full, tm.full, m.empty])
                        tk = tt(v3(m.a), v3(m.a), C("nincl").unsqueeze(1).broadcast_to([128, 4, 128]), ADD, [tk])
                        tk = act(m.a, m.a, ACT.Exp, [tk])
                        m.full = tt(m.a, m.a, cb.a, MUL, [tk, cb.full])
                        c = yield from SP.take()
                        tk = act(c.a, bA.a, ACT.Exp, [bA.full, c.empty])
                        PS.put(bA, A.now(), V.now())
                        c.full = tt(c.a, c.a, Cf[g].a, MUL, [tk, Cf[g].full])
                        ms.append(m)
                        cs.append(c)
                        yield
                    z = yield from dense("s_z", F, hk)
                    sz = yield from SP.take()
                    t2 = silu2(sz.a, z.a, [z.full, sz.empty])
                    PS.put(z, V.now())
                    Y = yield from PS.take()
                    for hh in range(2):
                        q = slice(64 * hh, 64 * hh + 64)
                        for t in range(4):
                            s = slice(t * 128, t * 128 + 128)
                            Y.full = mm(Y.a[q, s], v3(xd[F].a)[:, t, q], ms[hh].a[:, s], True, t == 0,
                                     [xd[F].full, ms[hh].full, Y.empty])
                            if t:
                                Y.full = mm(Y.a[q, s], st[t].a[:, f * 128 + hh * 64:f * 128 + hh * 64 + 64],
                                         cs[hh].a[:, s], False, True, [st[t].full, cs[hh].full])
                    for x in ms + cs:
                        SP.put(x, T.now())
                    tk = stt(xs[F].a, xs[F].a, P("ssm_d", F), Y.a, MUL, ADD, [xs[F].full, Y.full, T.now()])
                    PS.put(Y, V.now())
                    SP.put(xd[F], T.now())
                    xs[F].full = stt(xs[F].a, xs[F].a, 0.5, sz.a, MUL, MUL, [tk, t2])
                    SP.put(sz, V.now())
                    ys[F] = xs[F]

                yield from workers([channel(f) for f in range(4)], 3, 0, 6)
                SP.put(cb, V.now())
                SP.put(Cf[g], V.now(), T.now())
                for s in st[1:]:
                    SP.put(s, T.now(), V.now())
                tY = [y.full for y in ys[4 * g:4 * g + 4]]
                b = yield from token_squares(1, [y.a for y in ys[4 * g:4 * g + 4]], tY)
                r = yield from spread(b, 1, 1.0 / 512, 1e-6)
                tk = r.full
                for f in range(4):
                    y = ys[4 * g + f]
                    y.full = stt(y.a, y.a, P("ssm_norm_w", 4 * g + f), r.a, MUL, MUL, [tk, A.now()])
                PS.put(r, V.now())
                for f in range(4):
                    ys[4 * g + f] = yield from to_pair(ys[4 * g + f])
            ssm_y.extend(ys)

        def gdn_head(h, ys):
            cum, tm = K["cum"], K["tm"]
            qkv = []
            for i in range(3):
                b = yield from dense("g_qkv", 8 * i + h, hk)
                o = yield from SP.take()
                yield from conv(b, "gdn_conv_w", 8 * i + h, 24, o)
                qkv.append(o)
            q, k, v = qkv
            for s, mult in ((q, 128.0 ** -0.5), (k, 1.0)):
                b = yield from token_squares(1, [s.a], s.full)
                r = yield from spread(b, 1, 1.0, 1e-6, mult)
                s.full = tt(s.a, s.a, r.a, MUL, [r.full])
                PS.put(r, V.now())
            bG = yield from bc(cum.a, 32 + h, 64, cum.full)
            dec = yield from SP.take()
            t = tt(v3(dec.a), v3(bG.a), cols("tm", 32 + h, 33 + h).broadcast_to([128, 4, 128]), SUB,
                   [bG.full, tm.full, dec.empty])
            t = tt(v3(dec.a), v3(dec.a), C("nincl").unsqueeze(1).broadcast_to([128, 4, 128]), ADD, [t])
            dec.full = act(dec.a, dec.a, ACT.Exp, [t])
            qe = yield from SP.take()
            t = act(qe.a, bG.a, ACT.Exp, [bG.full, qe.empty])
            PS.put(bG, A.now(), V.now())
            qe.full = tt(qe.a, qe.a, q.a, MUL, [t, q.full])
            yield
            bB = yield from PS.take()
            bB.full = mm(bB.a, C("ident")[0:96, 64 + h:65 + h].to_broadcast([96, 128]), cum.a[0:96, :], True, True,
                      [cum.full, bB.empty])
            kb = yield from SP.take()
            kb.full = tt(kb.a, k.a, bB.a, MUL, [bB.full, k.full, kb.empty])
            PS.put(bB, V.now())
            yield
            bU = yield from PS.take()
            bQ = yield from PS.take()
            for t in range(4):
                s = slice(t * 128, t * 128 + 128)
                bU.full = mm(bU.a[:, s], k.a[:, s], kb.a[:, s], True, True, [kb.full, k.full, bU.empty])
            for t in range(4):
                s = slice(t * 128, t * 128 + 128)
                bQ.full = mm(bQ.a[:, s], k.a[:, s], q.a[:, s], True, True, [q.full, k.full, bQ.empty])
            SP.put(kb, T.now())
            U = yield from SP.take()
            t = tt(U.a, bU.a, dec.a, MUL, [bU.full, dec.full, U.empty])
            PS.put(bU, V.now())
            U.full = tt(v3(U.a), v3(U.a), C("strict").unsqueeze(1).broadcast_to([128, 4, 128]), MUL, [t])
            qk = dec
            qk.full = tt(dec.a, dec.a, bQ.a, MUL, [bQ.full, t])
            PS.put(bQ, V.now())
            SP.put(q, T.now(), V.now())
            yield
            TT = yield from invert(U, U.full, (16, 32, 64))
            SP.put(U, T.now(), G.now())
            bk = yield from transpose4(k.a, k.full)
            kd = yield from SP.take()
            vb = yield from SP.take()
            kd.full = tt(v3(kd.a), v3(bk.a), cols("end", 32 + h, 33 + h).broadcast_to([128, 4, 128]), MUL,
                      [bk.full, kd.empty, K["end"].full])
            PS.put(bk, V.now())
            bv = yield from transpose4(v.a, v.full)
            vb.full = tt(v3(vb.a), v3(bv.a), cols("tm", 64 + h, 65 + h).broadcast_to([128, 4, 128]), MUL,
                      [bv.full, vb.empty, tm.full])
            PS.put(bv, V.now())
            SP.put(v, T.now())
            nb = small(4).unsqueeze(2)
            t = ts(nb, cols("tm", 64 + h, 65 + h), -1.0, None, MUL, None, [tm.full])
            tn = tt(nb, nb, cols("ecum", 32 + h, 33 + h), MUL, [t, K["ecum"].full])
            yield
            O = yield from PS.take()
            sA = yield from SP.take()
            rv = yield from SP.take()
            tS = None
            for t in range(4):
                s = slice(t * 128, t * 128 + 128)
                St = sA.a[:, (t % 2) * 128:(t % 2) * 128 + 128]
                Sn = sA.a[:, (1 - t % 2) * 128:(1 - t % 2) * 128 + 128]
                b = yield from PS.take()
                if t:
                    b.full = mm(b.a[:, 0:128], k.a[:, s], St, True, True, [tS, b.empty])
                    tr = stt(rv.a[:, 0:128], b.a[:, 0:128], nb[:, t, :], vb.a[:, s], MUL, ADD,
                             [b.full, tn, vb.full])
                    R = rv.a[:, 0:128]
                    yield
                else:
                    R, tr = vb.a[:, s], vb.full
                tk = mm(b.a[:, 128:256], TT.a[:, s], R, True, True, [TT.full, tr, b.empty])
                vn = rv.a[:, 128 + 128 * (t % 2):256 + 128 * (t % 2)]
                tv = cp(vn, b.a[:, 128:256], [tk, rv.empty])
                yield
                O.full = mm(O.a[:, s], vn, qk.a[:, s], True, t == 0, [tv, qk.full, O.empty])
                if t:
                    O.full = mm(O.a[:, s], St, qe.a[:, s], False, True, [qe.full])
                if t < 3:
                    tk = mm(b.a[:, 256:384], kd.a[:, s], vn, True, True, [kd.full, tv])
                    if t == 0:
                        tS = cp(Sn, b.a[:, 256:384], [tk, sA.empty], V)
                    else:
                        tS = stt(Sn, St, cols("last", 32 + h, 33 + h)[:, t, :], b.a[:, 256:384], MUL, ADD,
                                 [tk, tS, K["last"].full])
                PS.put(b, V.now(), A.now())
                yield
            for s in (k, qe, kd, vb, qk, TT, sA, rv):
                SP.put(s, T.now(), V.now(), A.now())
            o = yield from SP.take()
            o.full = cp(o.a, O.a, [O.full, o.empty])
            PS.put(O, A.now())
            b = yield from token_squares(1, [o.a], o.full)
            r = yield from spread(b, 1, 1.0 / 128, 1e-6)
            t = stt(o.a, o.a, P("gdn_norm_w"), r.a, MUL, MUL, [r.full])
            PS.put(r, V.now())
            z = yield from dense("g_z", h, hk)
            sz = yield from SP.take()
            t2 = silu2(sz.a, z.a, [z.full, sz.empty])
            PS.put(z, V.now())
            o.full = stt(o.a, o.a, 0.5, sz.a, MUL, MUL, [t, t2])
            SP.put(sz, V.now())
            ys[h] = o

        ssm_y = []

        def gdn(ys, gates):
            yield from workers([gdn_head(h, ys) for h in range(8)] + [gate("gate_g", j, gates) for j in range(8)],
                               5, 2000.0, [12] * 8 + [1] * 8)

        def both(*gens, need=0):
            yield from workers(gens, len(gens), 0, need)

        running = []

        def workers(jobs, n, lag=0, need=0):
            jobs = list(jobs)
            needs = list(need) if isinstance(need, list) else [need] * len(jobs)
            live = []
            while jobs or live:
                while jobs and len(live) < n:
                    promised = sum(max(0, x[2]) for x in running)
                    if needs[0] and (live or running) and SP_free() - promised < needs[0]:
                        break
                    live.append([jobs.pop(0), T.clock + lag * len(live), needs.pop(0)])
                    if live[-1][2]:
                        running.append(live[-1])
                if not live:
                    yield -1.0
                    continue
                if dry:
                    now = T.clock + 250.0
                    k = min(range(len(live)), key=lambda i: (max(live[i][1], now), i))
                    picks.append(k)
                else:
                    k = picks.pop(0)
                me = live[k]
                had = SP_free()
                try:
                    r = next(me[0])
                    if r is None:
                        r = LAST[0]
                    elif r < 0:
                        r = max(T.clock, me[1]) + 500.0
                    me[1] = r
                    me[2] += SP_free() - had
                except StopIteration:
                    live[:] = [x for x in live if x is not me]
                    running[:] = [x for x in running if x is not me]
                    STEP[0] += 1
                if live:
                    yield min(x[1] for x in live)
                else:
                    yield

        def SP_free():
            return len(SP.free)

        def free_K():
            for s in K.values():
                SP.put(s, T.now(), V.now(), A.now())
            K.clear()

        def block1():
            yield from norm_h(lambda k: P("norm_mix_w", k))
            yield from ssm()
            ys, gates = [None] * 8, [None] * 8
            yield from both(gdn(ys, gates), branch("p_ssm", "gate_s", ssm_y, False), ada(), need=[0, 9, 1])
            for h in range(8):
                ys[h] = yield from to_pair(ys[h])
            yield from branch("p_gdn", "gate_g", ys, True, gates=gates)
            free_K()
            yield from merge("w_out")
            yield from ffn("norm_ffn_w", "ff_in", 0, "ff_in", 22, "ff_dn", None)
            r = yield from inv_rms(xk, tXX[0])
            for k in range(8):
                tXX[0] = stt(xk(k), xk(k), P("final_norm_w", k), r.a, MUL, MUL, [r.full, tP, tXX[0], A.now()])
            PS.put(r, V.now())
            yield

        def rwkv_pair(p, ys, wd):
            t1 = {}
            for n, i in (("r", p), ("k", 4 + p), ("v", 8 + p)):
                t1[n] = yield from shifted(i)
            r, k, v = t1["r"], t1["k"], t1["v"]
            up = [None, None]
            for i, (lo, bias) in enumerate(((0, "w0"), (64, "a0"))):
                b = yield from PS.take()
                b.full = mm(b.a, upw.a[lo:lo + 64, p * 128:p * 128 + 128], wd.a[lo:lo + 64, :], True, True,
                         [upw.full, wd.full, b.empty])
                o = yield from SP.take()
                o.full = tanh_half(o.a, b.a, [b.full, o.empty, tH], HP(bias, p))
                PS.put(b, A.now())
                up[i] = o
                yield
            lw, a = up
            t = ts(lw.a, lw.a, -0.5 * DECAY_SCALE, -0.5 * DECAY_SCALE, MUL, ADD, [lw.full])
            c = yield from SP.take()
            V.add(lambda e: e.tensor_tensor_scan(c.a, C("r64"), lw.a, 0.0, MUL, ADD), [t, tC, c.empty])
            c.full = V.now()
            kk = yield from SP.take()
            kk.full = ts(kk.a, k.a, P("k_k", p), None, MUL, None, [k.full, kk.empty])
            b = yield from token_squares(2, [kk.a], kk.full)
            rs = yield from spread(b, 2, None, None, floor=1e-24)
            kk.full = tt(kk.a, kk.a, rs.a, MUL, [rs.full])
            PS.put(rs, V.now())
            m = yield from SP.take()
            t = ts(m.a, a.a, 1.0, HP("k_a", p), SUB, MUL, [a.full, m.empty])
            t = ts(m.a, m.a, 1.0, None, ADD, None, [t])
            k.full = tt(k.a, k.a, m.a, MUL, [t, kk.full])
            a.full = stt(a.a, a.a, 1.0, kk.a, ADD, MUL, [t, kk.full])
            t = tt(m.a, r.a, k.a, MUL, [k.full, r.full])
            t = ts(m.a, m.a, P("r_k", p), None, MUL, None, [t])
            yield
            b = yield from PS.take()
            b.full = mm(b.a, C("blk"), m.a, True, True, [t, b.empty])
            m.full = tt(m.a, b.a, v.a, MUL, [b.full, v.full])
            PS.put(b, V.now())
            yield
            W = yield from SP.take()
            W.full = act(W.a, c.a, ACT.Exp, [c.full, W.empty])
            t = tt(lw.a, c.a, lw.a, SUB, [c.full])
            t = act(lw.a, lw.a, ACT.Exp, [t])
            kk.full = tt(kk.a, kk.a, lw.a, MUL, [t, a.full])
            SP.put(lw, V.now())
            r.full = tt(r.a, r.a, W.a, MUL, [W.full, V.now()])
            t = act(c.a, c.a, ACT.Exp, [V.now(), W.full], scale=-1.0)
            k.full = tt(k.a, k.a, c.a, MUL, [t, V.now()])
            a.full = stt(a.a, a.a, 0.5, c.a, MUL, MUL, [t, V.now()])
            SP.put(c, V.now())
            yield
            def mats(hh, L, R, msk):
                q = slice(64 * hh, 64 * hh + 64)
                b = yield from PS.take()
                for t in range(4):
                    s = slice(t * 128, t * 128 + 128)
                    b.full = mm(b.a[:, s], L.a[q, s], R.a[q, s], True, True, [L.full, R.full, b.empty])
                o = yield from SP.take()
                o.full = tt(v3(o.a), v3(b.a), C(msk).unsqueeze(1).broadcast_to([128, 4, 128]), MUL, [b.full, o.empty])
                PS.put(b, V.now())
                yield
                return o

            U = []
            for hh in range(2):
                U.append((yield from mats(hh, a, kk, "s64")))
            heads = []
            for hh in range(2):
                i = yield from invert(U[hh], U[hh].full, (16, 32))
                SP.put(U[hh], T.now(), G.now())
                heads.append([i])
            tok = []
            for s in (v, k, a):
                b = yield from transpose4(s.a, s.full)
                o = yield from SP.take()
                o.full = cp(o.a, b.a, [b.full, o.empty])
                PS.put(b, A.now())
                tok.append(o)
                if s is v:
                    SP.put(v, T.now(), V.now())
            vt, kt, bt = tok
            for hh in range(2):
                for L, R, msk in ((a, r, "i64"), (k, kk, "s64"), (k, r, "i64")):
                    heads[hh].append((yield from mats(hh, L, R, msk)))
            SP.put(k, T.now())
            SP.put(a, T.now())
            z = yield from SP.take()
            rs = yield from SP.take()
            step()
            t0 = G.add(lambda e: e.memset(z.a, 0.0), [z.empty])
            t0 = G.add(lambda e: e.memset(rs.a, 0.0), [rs.empty])
            Y = yield from PS.take()
            tZ = t0
            for c_ in range(8):
                tl, hf = c_ // 2, c_ % 2
                q = slice(64 * hf, 64 * hf + 64)
                sc = slice(c_ * 64, c_ * 64 + 64)
                s = slice(tl * 128, tl * 128 + 128)
                Zc = z.a[:, 128 * (c_ % 2):128 * (c_ % 2) + 128]
                Zn = z.a[:, 128 * ((c_ + 1) % 2):128 * ((c_ + 1) % 2) + 128]
                b = yield from PS.take()
                tk = mm(b.a[q, 0:128], kk.a[:, sc], Zc, True, False, [kk.full, tZ, b.empty])
                for hh in range(2):
                    cs = slice(64 * hh, 64 * hh + 64)
                    tk = mm(b.a[q, cs], heads[hh][2].a[:, sc], v3(vt.a)[:, tl, cs], False, hh == 1,
                            [heads[hh][2].full, vt.full])
                tr = cp(rs.a[q, 0:128], b.a[q, 0:128], [tk, t0])
                yield
                for hh in range(2):
                    cs = slice(64 * hh, 64 * hh + 64)
                    tk = mm(b.a[q, 128 + 64 * hh:192 + 64 * hh], heads[hh][0].a[:, sc],
                            rs.a[:, cs], True, True, [heads[hh][0].full, tr])
                tn = ts(rs.a[q, 128:256], b.a[q, 128:256], -1.0, None, MUL, None, [tk, t0])
                yield
                Y.full = mm(Y.a[:, sc], Zc, r.a[:, sc], True, False, [r.full, Y.empty])
                for hh in range(2):
                    hs = slice(64 * hh, 64 * hh + 64)
                    Y.full = mm(Y.a[hs, sc], v3(vt.a)[:, tl, hs], heads[hh][3].a[:, sc], False, False,
                             [heads[hh][3].full])
                    Y.full = mm(Y.a[hs, sc], rs.a[:, 128 + 64 * hh:192 + 64 * hh], heads[hh][1].a[:, sc], False, True,
                             [heads[hh][1].full, tn])
                yield
                if c_ < 7:
                    b2 = yield from PS.take()
                    mm(b2.a[:, 0:128], v3(kt.a)[q, tl, :], v3(vt.a)[q, tl, :], True, False, [kt.full, b2.empty])
                    tk = mm(b2.a[:, 0:128], v3(bt.a)[q, tl, :], rs.a[q, 128:256], False, True, [bt.full, tn])
                    wl = W.a[:, c_ * 64 + 63:c_ * 64 + 64]
                    for hh in range(2):
                        hs = slice(64 * hh, 64 * hh + 64)
                        t = tt(Zn[hs, hs], Zc[hs, hs], b2.a[hs, hs], ADD, [tk, tZ])
                        tZ_ = ts(Zn[hs, hs], Zn[hs, hs], wl[hs], None, MUL, None, [t, W.full])
                    tZ = tZ_
                    PS.put(b2, V.now())
                PS.put(b, V.now(), A.now())
                yield
            for hd in heads:
                for x in hd:
                    SP.put(x, T.now())
            for x in (kk, r, W, kt, bt, vt, z, rs):
                SP.put(x, T.now(), V.now(), A.now())
            y = yield from SP.take()
            y.full = cp(y.a, Y.a, [Y.full, y.empty])
            PS.put(Y, A.now())
            yield
            b = yield from PS.take()
            b.full = mm(b.a, C("blk"), y.a, True, True, [y.full, b.empty])
            y.full = stt(y.a, b.a, -1.0 / 64, y.a, MUL, ADD, [b.full])
            PS.put(b, V.now())
            b = yield from token_squares(2, [y.a], y.full)
            b = yield from spread(b, 2, 1.0 / 64, 64e-5)
            t = stt(y.a, y.a, P("gn_w", p), b.a, MUL, MUL, [b.full])
            PS.put(b, V.now())
            g = yield from shifted(13 + p)
            rr = yield from SP.take()
            tg = silu2(rr.a, g.a, [g.full, rr.empty])
            t = stt(y.a, y.a, P("gn_b", p), m.a, ADD, ADD, [t, m.full])
            y.full = stt(y.a, y.a, 0.5, rr.a, MUL, MUL, [t, tg])
            SP.put(rr, V.now())
            SP.put(m, V.now())
            SP.put(g, V.now(), A.now())
            ys[p] = yield from to_pair(y)

        def shifted(i):
            b = yield from dense("pa", i, hk)
            o = yield from SP.take()
            t = ts(o.a, b.a, omu[:, i:i + 1], None, MUL, None, [b.full, o.empty, tomu[0]])
            o.full = stt(o.a[:, 1:512], b.a[:, 0:511], P("mu", i), o.a[:, 1:512], MUL, ADD, [t])
            PS.put(b, V.now())
            return o

        omu = small(17)
        tomu = [None]
        upw = None

        def rwkv(ys):
            nonlocal upw
            upw = yield from SP.take()
            load(upw, upw.a[0:64, :], D["up"][0:64, 0, :])
            load(upw, upw.a[64:128, :], D["up"][64:128, 1, :])
            wd = yield from shifted(12)
            wd.full = [wd.full, act(wd.a[0:64], wd.a[0:64], ACT.Tanh, [wd.full])]
            return wd

        def head_rms(s, gain):
            b = yield from token_squares(2, [s.a], s.full)
            r = yield from spread(b, 2, 1.0 / 64, 1e-6)
            s.full = stt(s.a, s.a, P(gain), r.a, MUL, MUL, [r.full])
            PS.put(r, V.now())

        def plain(name, j):
            b = yield from dense(name, j, hk)
            o = yield from SP.take()
            o.full = cp(o.a, b.a, [b.full, o.empty])
            PS.put(b, A.now())
            yield
            return o

        def index(masks):
            ik = yield from plain("ik", 0)
            iq = []
            for j in range(4):
                iq.append((yield from plain("iq", j)))
            b = yield from dense("iw", 0, hk)
            x = yield from SP.take()
            t = cp(x.a[0:8, :], b.a[0:8, :], [b.full, x.empty])
            PS.put(b, A.now())
            b = yield from PS.take()
            for m in range(4):
                b.full = tp(b.a[:, m * 8:m * 8 + 8], x.a[0:8, m * 128:m * 128 + 128], [t, b.empty], n=8)
            SP.put(x, T.now())
            iw = small(32)
            tw = ts(iw, b.a[:, 0:32], 8.0 ** -0.5, None, MUL, None, [b.full])
            PS.put(b, V.now())
            mx = small(8)
            for qb in range(1, 4):
                W = 128 * (qb + 1)
                acc = yield from SP.take()
                for h in range(8):
                    q = slice(64 * (h % 2), 64 * (h % 2) + 64)
                    b = yield from PS.take()
                    b.full = mm(b.a[:, 0:W], iq[h // 2].a[q, qb * 128:qb * 128 + 128], ik.a[q, 0:W], True, True,
                             [iq[h // 2].full, ik.full, b.empty])
                    rl = yield from SP.take()
                    t = act(rl.a[:, 0:W], b.a[:, 0:W], ACT.Relu, [b.full, rl.empty], scale=0.125)
                    PS.put(b, A.now())
                    w = iw[:, qb * 8 + h:qb * 8 + h + 1]
                    if h == 0:
                        acc.full = ts(acc.a[:, 0:W], rl.a[:, 0:W], w, None, MUL, None, [t, tw, acc.empty])
                    else:
                        acc.full = stt(acc.a[:, 0:W], rl.a[:, 0:W], w, acc.a[:, 0:W], MUL, ADD, [t, acc.full])
                    SP.put(rl, V.now())
                    yield
                step()
                t = V.add(lambda e, o=acc.a[0:64, W - 64:W]: e.memset(o, -2.0e38), [acc.full])
                for r in range(16):
                    t = V.add(lambda e, o=acc.a[:, 0:W]: e.max(mx, o), [t])
                    t = V.add(lambda e, o=acc.a[:, 0:W]: e.match_replace(o, mx, o, -3.0e38), [t])
                    step()
                    yield
                t = ts(acc.a[:, 0:W], acc.a[:, 0:W], -2.5e38, NEG, ALU.is_gt, MUL, [t])
                acc.full = t
                masks[qb] = acc
            for s in iq + [ik]:
                SP.put(s, T.now())
            m0 = yield from SP.take()
            step()
            G.add(lambda e: e.memset(m0.a[:, 0:128], 0.0), [m0.empty])
            m0.full = G.add(lambda e: e.memset(m0.a[0:64, 64:128], NEG), [G.now()])
            masks[0] = m0

        def dsa(masks, ys):
            def job(f):
                while None in masks:
                    yield -1.0
                b = yield from by_token("qkv2", 8 + f)
                v = yield from SP.take()
                v.full = cp(v.a, b.a, [b.full, v.empty])
                PS.put(b, A.now())
                q = yield from plain("qkv2", f)
                k = yield from plain("qkv2", 4 + f)
                yield from head_rms(q, "q_gain")
                yield from head_rms(k, "k_gain")
                O = yield from PS.take()
                yield from both(*[dsa_head(q, k, v, hh, masks, O) for hh in range(2)])
                tO = T.now()
                SP.put(q, T.now())
                SP.put(k, T.now())
                SP.put(v, T.now())
                o = yield from SP.take()
                g = yield from dense("gb", f, hk)
                t = silu2(o.a, g.a, [g.full, o.empty])
                PS.put(g, V.now())
                o.full = stt(o.a, o.a, 0.5, O.a, MUL, MUL, [t, tO])
                PS.put(O, V.now())
                ys[f] = yield from to_pair(o)

            return [job(f) for f in range(4)]

        def softmax(ps, W, mask, tmask, scale, e, col):
            t = V.add(lambda n: n.tensor_tensor_reduce(e.a[:, 0:W], ps.a[:, 0:W], mask, 1.0, -3.0e38, ADD, MAX,
                                                       col[:, 0:1]), [ps.full, tmask, e.empty])
            step()
            PS.put(ps, V.now())
            t = ts(col[:, 0:1], col[:, 0:1], -scale, None, MUL, None, [t])
            return act(e.a[:, 0:W], e.a[:, 0:W], ACT.Exp, [t], bias=col[:, 0:1], scale=scale,
                       accum_out=col[:, 1:2])

        def dsa_head(q, k, v, hh, masks, O):
            hs = slice(64 * hh, 64 * hh + 64)
            col = small(2)
            for qb in range(4):
                W = 128 * (qb + 1)
                b = yield from PS.take()
                b.full = mm(b.a[:, 0:W], q.a[hs, qb * 128:qb * 128 + 128], k.a[hs, 0:W], True, True, [q.full, k.full, b.empty])
                e = yield from SP.take()
                t = softmax(b, W, masks[qb].a[:, 0:W], masks[qb].full, 0.125, e, col)
                t = V.add(lambda n: n.reciprocal(col[:, 1:2], col[:, 1:2]), [t])
                t = ts(e.a[:, 0:W], e.a[:, 0:W], col[:, 1:2], None, MUL, None, [t])
                yield
                yield from pv(e, t, qb, lambda s: v3(v.a)[:, s, hs], v.full, O, hs)

        def pv(e, te, qb, vf, tv, O, hs):
            yield
            b = yield from PS.take()
            for s in range(qb + 1):
                t = tp(b.a[:, s * 128:s * 128 + 128], e.a[:, s * 128:s * 128 + 128], [te, b.empty])
            SP.put(e, T.now())
            et = yield from SP.take()
            t = cp(et.a[:, 0:128 * (qb + 1)], b.a[:, 0:128 * (qb + 1)], [t, et.empty])
            PS.put(b, A.now())
            yield
            for s in range(qb + 1):
                mm(O.a[hs, qb * 128:qb * 128 + 128], vf(s), et.a[:, s * 128:s * 128 + 128], s == 0, s == qb,
                   [t, tv, O.empty])
            SP.put(et, T.now())
            yield

        mod = small(24)
        tmod = [None]

        def ada():
            cs = small(8)
            t = silu2(cs, PC[:, PAT["c"][0]:PAT["c"][1]], [tP])
            t = ts(cs, cs, 0.5, None, MUL, None, [t])
            b = yield from PS.take()
            for j in range(24):
                if j % 4 == 0:
                    row = yield from PS.take()
                w, wa, _ = panel("ada", j, 0, 8, 128)
                o = (j % 4) * 128
                for k in range(8):
                    tk = mm(row.a[0:1, o:o + 128], cs[:, k:k + 1], wa[:, k, :], k == 0, k == 7, [w.full, t, row.empty])
                WR.put(w, T.now())
                yield T.clock + 3000.0
                if j % 4 == 3:
                    x = yield from SP.take()
                    tr = cp(x.a[0:1, :], row.a[0:1, :], [tk, x.empty])
                    PS.put(row, A.now())
                    yield
                    for i in range(4):
                        tk = mm(b.a[:, j - 3 + i:j - 2 + i], x.a[0:1, i * 128:i * 128 + 128],
                                C("ones")[0:1, 0:1], True, True, [tr, b.empty, tC])
                    SP.put(x, T.now())
            tmod[0] = tt(mod, b.a[:, 0:24], PC[:, PAT["b_ada"][0]:PAT["b_ada"][1]], ADD, [tk])
            PS.put(b, V.now())

        def block2():
            tm = tmod[0]
            gc = small(8)
            t = ts(gc, mod[:, 8:16], 1.0, None, ADD, None, [tm])
            t = tt(gc, gc, PC[:, PAT["norm_w"][0]:PAT["norm_w"][1]], MUL, [t])
            hm = small(8)
            t = [t, ts(hm, mod[:, 16:24], 0.5, None, MUL, None, [tm])]
            tomu[0] = ts(omu, PC[:, PAT["mu"][0]:PAT["mu"][1]], -1.0, 1.0, MUL, ADD, [tP])
            tXX[0] = [tXX[0], t]
            yield from norm_h(lambda k: gc[:, k:k + 1], shift=lambda k: mod[:, k:k + 1])
            masks = [None] * 4
            yr, yd, gates = [None] * 4, [None] * 4, [None] * 8
            ga = [None] * 8

            def pairs():
                wd = yield from rwkv(yr)

                def last():
                    while None in yr:
                        yield -1.0
                    SP.put(upw, T.now())
                    SP.put(wd, T.now())
                    yield from branch("a_out", "gm", yr, False, gates=ga)

                rp = [rwkv_pair(p, yr, wd) for p in range(4)]
                yield from workers(rp[0:2] + [gate("gm", j, ga) for j in range(NG)] + rp[2:4]
                                   + dsa(masks, yd) + [last()] + [gate("gm", 8 + j, gates) for j in range(8)],
                                   4, 0, [17] * 2 + [1] * NG + [17] * 2 + [9] * 4 + [9 - NG] + [1] * 8)
                for s in masks:
                    SP.put(s, T.now(), V.now())

            yield from both(index(masks), pairs(), need=[10, 0])
            yield from branch("b_out", "gm", yd, True, gofs=8, gates=gates)
            yield from merge("w_o", col=lambda j: hm[:, j:j + 1])

        def gmlp():
            ld = []
            for n in range(2):
                s = yield from SP.take()
                load(s, s.a, D["lnp"][:, n, :])
                ld.append(s)
            bs = yield from SP.take()
            load(bs, bs.a, D["bs"].rearrange("p a b -> p (a b)"))
            ws = []
            for n in range(2):
                s = yield from SP.take()
                load(s, s.a, D["wsT"][:, 4 * n:4 * n + 4, :].rearrange("p a b -> p (a b)"))
                s.full = tt(v3(s.a), v3(s.a), C("incl").unsqueeze(1).broadcast_to([128, 4, 128]), MUL, [s.full, tC])
                ws.append(s)
            vt = []
            for m in range(4):
                vt.append((yield from SP.take()))
            for j in range(4):
                b = yield from by_token("in3", 20 + j, ACT.Gelu)
                for m in range(4):
                    vt[m].full = cp(vt[m].a[:, j * 128:j * 128 + 128], b.a[:, m * 128:m * 128 + 128],
                                 [b.full, vt[m].empty])
                PS.put(b, A.now())
            for m in range(4):
                c = small(6)
                t = V.add(lambda e, o=c, x=vt[m]: e.tensor_reduce(o[:, 0:1], x.a, AX.X, ADD), [vt[m].full])
                t = ts(c[:, 0:1], c[:, 0:1], -1.0 / 512, None, MUL, None, [t])
                t = ts(vt[m].a, vt[m].a, c[:, 0:1], None, ADD, None, [t])
                q = yield from SP.take()
                t = act(q.a, vt[m].a, ACT.Square, [t, q.empty], accum_out=c[:, 1:2])
                SP.put(q, A.now())
                t = ts(c[:, 2:3], c[:, 1:2], 1.0 / 512, 1e-5, MUL, ADD, [t])
                t = newton(c[:, 2:3], c[:, 3:4], c[:, 4:5], c[:, 5:6], t, 1.0)
                t = stt(vt[m].a, vt[m].a, c[:, 4:5], ld[0].a, MUL, MUL, [t, ld[0].full])
                vt[m].full = tt(vt[m].a, vt[m].a, ld[1].a, ADD, [t, ld[1].full])
                yield
            ys = []
            for f in range(4):
                b = yield from PS.take()
                for hh in range(2):
                    g = 2 * f + hh
                    for m in range(4):
                        b.full = mm(b.a[64 * hh:64 * hh + 64, m * 128:m * 128 + 128],
                                 vt[m].a[:, g * 64:g * 64 + 64], v3(ws[g // 4].a)[:, g % 4, :], True, True,
                                 [vt[m].full, ws[g // 4].full, b.empty])
                u = yield from dense("in3", 16 + f, hk)
                o = yield from SP.take()
                t = act(o.a, u.a, ACT.Gelu, [u.full, o.empty])
                PS.put(u, A.now())
                q = yield from SP.take()
                t2 = tt(v3(q.a), v3(b.a), v3(bs.a)[:, f, :].unsqueeze(1).broadcast_to([128, 4, 128]), ADD,
                        [b.full, bs.full, q.empty])
                PS.put(b, V.now())
                o.full = tt(o.a, o.a, q.a, MUL, [t, t2])
                SP.put(q, V.now())
                ys.append((yield from to_pair(o)))
            for s in ld + ws + vt + [bs]:
                SP.put(s, T.now(), V.now())
            yield from branch("a_proj", "in3", ys, False)

        def rope():
            pi = yield from SP.take()
            load(pi, pi.a.bitcast(I32), D["pos"])
            an = yield from SP.take()
            t = V.add(lambda e: e.tensor_copy(an.a, pi.a.bitcast(I32)), [pi.full, an.empty])
            t = ts(an.a, an.a, C("freq"), None, MUL, None, [t, tC])
            SP.put(pi, V.now())
            tw = 2.0 * math.pi
            c1 = 6.28125
            c2 = float(np.float32(np.round((tw - c1) * 2 ** 21) / 2 ** 21))
            c3 = float(tw - c1 - c2)
            big = 12582912.0
            res = []
            for ofs in (0.25, 0.0):
                n = yield from SP.take()
                o = yield from SP.take()
                t1 = ts(n.a, an.a, 1.0 / tw, ofs, MUL, ADD, [t, n.empty])
                t1 = ts(n.a, n.a, big, None, ADD, None, [t1])
                t1 = ts(n.a, n.a, big, None, SUB, None, [t1])
                t1 = stt(o.a, n.a, -c1, an.a, MUL, ADD, [t1, o.empty])
                t1 = stt(o.a, n.a, -c2, o.a, MUL, ADD, [t1])
                t1 = stt(o.a, n.a, -c3, o.a, MUL, ADD, [t1])
                if ofs:
                    t1 = ts(o.a, o.a, math.pi / 2, None, ADD, None, [t1])
                t1 = ts(o.a, o.a, 3.1415925, -3.1415925, MIN, MAX, [t1])
                o.full = act(o.a, o.a, ACT.Sin, [t1])
                SP.put(n, V.now())
                res.append(o)
            SP.put(an, V.now())
            return res

        def rope_apply(s, cs, sn):
            yield
            b = yield from PS.take()
            b.full = mm(b.a, C("rot"), s.a, True, True, [s.full, b.empty])
            q = yield from SP.take()
            t = tt(q.a, b.a, sn.a, MUL, [b.full, sn.full, q.empty])
            PS.put(b, V.now())
            t2 = tt(s.a, s.a, cs.a, MUL, [cs.full, b.full])
            s.full = tt(s.a, s.a, q.a, ADD, [t, t2])
            SP.put(q, V.now())

        def diff(ys, gates):
            cs, sn = yield from rope()
            l = yield from SP.take()
            load(l, l.a[:, 0:256], D["lam"].rearrange("p a b -> p (a b)"))
            c = small(4)
            t = tt(l.a[:, 256:320], l.a[:, 0:64], l.a[:, 64:128], MUL, [l.full])
            t = tt(l.a[:, 320:384], l.a[:, 128:192], l.a[:, 192:256], MUL, [l.full])
            t = V.add(lambda e: e.tensor_reduce(c[:, 0:2], l.a[:, 256:384].rearrange("p (a b) -> p a b", a=2),
                                                AX.X, ADD), [V.now()])
            t = act(c[:, 0:2], c[:, 0:2], ACT.Exp, [t])
            t = tt(c[:, 2:3], c[:, 1:2], c[:, 0:1], SUB, [t])
            tl = ts(c[:, 2:3], c[:, 2:3], LAM_INIT, None, SUB, None, [t])
            SP.put(l, V.now())
            nlam = c[:, 2:3]

            def head(h):
                b = yield from by_token("in3", 40 + h)
                v = yield from SP.take()
                v.full = cp(v.a, b.a, [b.full, v.empty])
                PS.put(b, A.now())
                q = yield from plain("in3", 24 + h)
                k = yield from plain("in3", 32 + h)
                yield from head_rms(q, "b_q_norm")
                yield from head_rms(k, "b_k_norm")
                yield from rope_apply(q, cs, sn)
                yield from rope_apply(k, cs, sn)
                O = yield from PS.take()
                col = small(4)
                for qb in range(4):
                    W = 128 * (qb + 1)
                    es = []
                    for m in range(2):
                        hs = slice(64 * m, 64 * m + 64)
                        b = yield from PS.take()
                        b.full = mm(b.a[:, 0:W], q.a[hs, qb * 128:qb * 128 + 128], k.a[hs, 0:W], True, True,
                                 [q.full, k.full, b.empty])
                        e = yield from SP.take()
                        e.full = softmax(b, W, C("causal")[:, 512 - W:512], tC, 0.125, e, col[:, 2 * m:2 * m + 2])
                        es.append(e)
                        yield
                    t = V.add(lambda n: n.reciprocal(col[:, 1:2], col[:, 1:2]), [es[0].full])
                    t1 = V.add(lambda n: n.reciprocal(col[:, 3:4], col[:, 3:4]), [es[1].full])
                    t1 = ts(col[:, 3:4], col[:, 3:4], nlam, None, MUL, None, [t1, tl])
                    t = ts(es[0].a[:, 0:W], es[0].a[:, 0:W], col[:, 1:2], None, MUL, None, [t])
                    t = stt(es[0].a[:, 0:W], es[1].a[:, 0:W], col[:, 3:4], es[0].a[:, 0:W], MUL, ADD, [t, t1])
                    SP.put(es[1], V.now())
                    yield from pv(es[0], t, qb, lambda s: v3(v.a)[:, s, :], v.full, O, slice(0, 128))
                SP.put(q, T.now())
                SP.put(k, T.now())
                SP.put(v, T.now())
                o = yield from SP.take()
                o.full = cp(o.a, O.a, [T.now(), o.empty])
                PS.put(O, A.now())
                oc = yield from SP.take()
                od = yield from SP.take()
                tc = ts(oc.a, o.a, 1e18, -1e18, MIN, MAX, [o.full, oc.empty])
                td = ts(od.a, o.a, 2.0 ** -70, None, MUL, None, [o.full, od.empty])
                b = yield from colsum("ones", [oc.a], tc)
                b2 = yield from colsum("ones", [od.a], td)
                fin = oc
                tf = ts(fin.a, b2.a, 2.0 ** -12, None, ALU.is_lt, None, [b2.full, T.now()])
                t = ts(od.a, b2.a, 2.0 ** -12 * (1 - 2.0 ** -22), 2.0 ** 70, MIN, MUL, [b2.full, T.now(), A.now()])
                t = ts(od.a, od.a, 2.0 ** 70, None, MUL, None, [t])
                t = tt(od.a, od.a, b.a, MAX, [t, b.full])
                PS.put(b, V.now())
                PS.put(b2, V.now())
                r = yield from SP.take()
                t = rsq(r.a, od.a, 1.0 / 128, 1e-6, 1.0 - LAM_INIT, [t, r.empty])
                t = tt(r.a, r.a, fin.a, MUL, [t, tf])
                SP.put(oc, V.now())
                SP.put(od, V.now())
                o.full = stt(o.a, r.a, P("subln"), o.a, MUL, MUL, [t])
                SP.put(r, V.now())
                ys[h] = o

            yield from workers([head(h) for h in range(8)] + [gate("in3", 8 + j, gates) for j in range(8)],
                               4, 1000.0, [8] * 8 + [1] * 8)
            SP.put(cs, V.now())
            SP.put(sn, V.now())

        def block3():
            yield from ffn("ffn1_norm", "f1g", 0, "f1u", 0, "f1d", 0.5)
            yield from norm_h(lambda k: P("mix_norm", k))
            ys, gates = [None] * 8, [None] * 8
            yield from both(diff(ys, gates), gmlp(), need=[0, 26])
            for h in range(8):
                ys[h] = yield from to_pair(ys[h])
            yield from branch("b_proj", "in3", ys, True, gofs=8, gates=gates)
            yield from merge("out3")
            yield from ffn("ffn2_norm", "f2g", 0, "f2u", 0, "f2d", 0.5, sq=False)

        def whole():
            yield from block1()
            yield from block2()
            yield from block3()

        run(whole())
        S.q.append(([V.now()], lambda e: e.dma_start(out, X[:, :, :]), s_o, 16))
        assert dry or not picks
        return asked, picks, T, V, A, G, S


def lay(W):
    K, N = W.shape
    return np.ascontiguousarray(W.reshape(K // 128, 128, N // 128, 128).transpose(2, 1, 0, 3))


def lay_small(W, n):
    return np.ascontiguousarray(W.reshape(8, 128, n).transpose(1, 0, 2))[None]


def col(v):
    return v.reshape(-1, 128).T


def layout(I):
    A = {}
    w = I["w_in"][0]
    o = np.cumsum([0, 1024, 1536, 16, 3072, 1024, 8, 8, 1024, 1024])
    part = [w[:, o[i]:o[i + 1]] for i in range(9)]
    A["s_z"], A["s_xbc"], A["g_qkv"], A["g_z"] = lay(part[0]), lay(part[1]), lay(part[3]), lay(part[4])
    A["gate_s"], A["gate_g"] = lay(part[7]), lay(part[8])
    sm = np.zeros((1024, 96), np.float32)
    sm[:, 0:16], sm[:, 32:40], sm[:, 64:72] = part[2], part[5], part[6]
    A["small"] = lay_small(sm, 96)
    A["p_ssm"], A["p_gdn"], A["w_out"] = lay(I["w_proj_ssm"][0]), lay(I["w_proj_gdn"][0]), lay(I["w_out"][0])
    A["ff_in"], A["ff_dn"] = lay(I["w_ffn_in"][0]), lay(I["w_ffn_down"][0])
    A["ada"] = lay(I["w_ada_2"][0])
    w = I["w_in_2"][0]
    A["pa"] = lay(w[:, 0:2176])
    A["qkv2"] = lay(w[:, 2176:3712])
    A["gb"] = lay(w[:, 3712:4224])
    A["iq"] = lay(w[:, 4224:4736])
    A["ik"] = lay(np.concatenate([w[:, 4736:4800], w[:, 4736:4800]], axis=1))
    A["iw"] = lay_small(np.ascontiguousarray(w[:, 4800:4808]), 8)
    A["gm"] = lay(w[:, 4808:6856])
    A["a_out"], A["b_out"], A["w_o"] = lay(I["w_a_out_2"][0]), lay(I["w_b_out_2"][0]), lay(I["w_o_2"][0])
    A["f1g"], A["f1u"], A["f1d"] = (lay(I[f"ffn1_w_{n}_3"][0]) for n in ("gate", "up", "down"))
    A["f2g"], A["f2u"], A["f2d"] = (lay(I[f"ffn2_w_{n}_3"][0]) for n in ("gate", "up", "down"))
    A["in3"] = lay(I["w_in_3"][0])
    A["a_proj"], A["b_proj"], A["out3"] = lay(I["a_w_proj_3"][0]), lay(I["b_w_proj_3"][0]), lay(I["w_out_3"][0])
    A["lnp"] = np.ascontiguousarray(np.broadcast_to(
        np.stack([I["a_ln_gain_3"][0], I["a_ln_bias_3"][0]])[None], (128, 2, 512)))
    bs = I["a_b_s_3"][0]
    A["bs"] = np.ascontiguousarray(np.repeat(bs.reshape(4, 2, 1, 128), 64, axis=2).reshape(4, 128, 128)
                                   .transpose(1, 0, 2))
    A["wsT"] = np.ascontiguousarray(I["a_w_s_3"][0].transpose(2, 0, 1))
    A["lam"] = np.ascontiguousarray(np.broadcast_to(np.stack(
        [I[f"b_lambda_{n}_3"][0] for n in ("q1", "k1", "q2", "k2")])[None], (128, 4, 64)))
    up = np.zeros((128, 2, 512), np.float32)
    up[0:64, 0] = I["w_up_2"][0]
    up[64:128, 1] = I["a_up_2"][0]
    A["up"] = up
    A["pos"] = np.ascontiguousarray(np.broadcast_to(I["positions_3"], (128, 512)))
    A["x"] = np.ascontiguousarray(I["x"][0].T.reshape(8, 128, 512).transpose(1, 0, 2))

    z = np.zeros(128, np.float32)
    dtb, alog = z.copy(), z.copy()
    dtb[0:16], dtb[32:40] = I["ssm_dt_bias"][0], I["gdn_dt_bias"][0]
    alog[0:16], alog[32:40] = I["ssm_a_log"][0], I["gdn_a_log"][0]
    two = np.tile
    P = {
        "norm_mix_w": col(I["norm_mix_w"][0]), "ssm_conv_w": col(I["ssm_conv_w"][0].reshape(-1)),
        "ssm_conv_b": col(I["ssm_conv_b"][0]), "dtb": col(dtb), "alog": col(alog),
        "ssm_d": col(np.repeat(I["ssm_d"][0], 64)), "ssm_norm_w": col(I["ssm_norm_w"][0]),
        "gdn_conv_w": col(I["gdn_conv_w"][0].reshape(-1)), "gdn_norm_w": col(I["gdn_norm_w"][0]),
        "norm_ffn_w": col(I["norm_ffn_w"][0]), "final_norm_w": col(I["final_norm_w"]),
        "c": col(I["c_2"][0]), "norm_w": col(I["norm_w_2"][0]), "b_ada": col(I["b_ada_2"][0]),
        "mu": col(I["mu_2"][0]), "w0": col(I["w0_2"][0]), "a0": col(I["a0_2"][0]), "k_k": col(I["k_k_2"][0]),
        "k_a": col(I["k_a_2"][0]), "r_k": col(I["r_k_2"][0].reshape(-1)), "gn_w": col(I["gn_w_2"][0]),
        "gn_b": col(I["gn_b_2"][0]), "q_gain": col(two(I["q_gain_2"][0], 2)), "k_gain": col(two(I["k_gain_2"][0], 2)),
        "ffn1_norm": col(I["ffn1_norm_3"][0]), "mix_norm": col(I["mix_norm_3"][0]),
        "b_q_norm": col(two(I["b_q_norm_3"][0], 2)), "b_k_norm": col(two(I["b_k_norm_3"][0], 2)),
        "subln": col(I["b_subln_3"][0]), "ffn2_norm": col(I["ffn2_norm_3"][0]),
    }
    A["params"] = np.ascontiguousarray(np.concatenate([P[k] for k, _ in PCOLS], axis=1))
    A["consts"] = constants()[0]
    return A


def kernel(**inputs):
    import concourse.bacc as bacc
    from concourse.bass_utils import run_bass_kernel_spmd

    arrays = layout({k: np.asarray(v) for k, v in inputs.items()})
    nc = bacc.Bacc("TRN2", target_bir_lowering=False, num_devices=1)
    D = {n: nc.dram_tensor(f"in_{n}", a.shape, mybir.dt.from_np(a.dtype), kind="ExternalInput").ap()
         for n, a in arrays.items()}
    out = nc.dram_tensor("out_x", (128, 8, 512), F32, kind="ExternalOutput").ap()
    build(nc, D, out)
    r = run_bass_kernel_spmd(nc, [{f"in_{n}": a for n, a in arrays.items()}], core_ids=[0])
    y = r.results[0]["out_x"]
    return np.ascontiguousarray(y.transpose(1, 0, 2).reshape(1024, 512).T)[None]
```
